# Optimizing a Trainium2 kernel written in Bass

```python
import jax, jax.numpy as jnp
from jax import lax
import numpy as np

D_MODEL = 1024
BATCH = 1
SEQ = 1024
DEPTH = 1

N_HEADS = 8
QK_NOPE_DIM = 64
QK_ROPE_DIM = 32
QK_DIM = QK_NOPE_DIM + QK_ROPE_DIM
V_DIM = 64
Q_LORA = 256
KV_LORA = 256
ROPE_THETA = 10000.0
Q_BLOCK = 128
F_GROUPS = 4
F_GROUP_DIM = 128
F_DIM = F_GROUPS * F_GROUP_DIM
N_BRANCH = 2
IN_DIM = Q_LORA + KV_LORA + QK_ROPE_DIM + F_DIM + N_BRANCH * D_MODEL
SPLITS = (Q_LORA, Q_LORA + KV_LORA, Q_LORA + KV_LORA + QK_ROPE_DIM, Q_LORA + KV_LORA + QK_ROPE_DIM + F_DIM)
PEER_HEADS = 8
PEER_NKEYS = 128
PEER_EXPERTS = PEER_NKEYS * PEER_NKEYS
PEER_QDIM = 256
PEER_HALF = PEER_QDIM // 2
PEER_TOPK = 16
PEER_CHUNK = 128
DN_ALPHA = (2.0 * DEPTH) ** 0.25
DN_BETA = (8.0 * DEPTH) ** -0.25
LN_EPS = 1e-5
RMS_EPS = 1e-6

kernel_name = "hybrid_mla_fnet_peer_deepnorm_encoder"

def layer_norm(x, g, b):
    xf = x.astype(jnp.float32)
    mu = jnp.mean(xf, axis=-1, keepdims=True)
    var = jnp.mean(jnp.square(xf - mu), axis=-1, keepdims=True)
    y = (xf - mu) * lax.rsqrt(var + LN_EPS) * g.astype(jnp.float32) + b.astype(jnp.float32)
    return y.astype(x.dtype)

def rms_norm(x, g):
    xf = x.astype(jnp.float32)
    y = xf * lax.rsqrt(jnp.mean(jnp.square(xf), axis=-1, keepdims=True) + RMS_EPS) * g.astype(jnp.float32)
    return y.astype(x.dtype)

def rotary_tables(seq_len):
    pos = jnp.arange(seq_len, dtype=jnp.float32)
    inv = 1.0 / (ROPE_THETA ** (jnp.arange(0, QK_ROPE_DIM, 2, dtype=jnp.float32) / QK_ROPE_DIM))
    ang = pos[:, None] * inv[None, :]
    return jnp.cos(ang), jnp.sin(ang)

def apply_rope(x, cos, sin):
    xf = x.astype(jnp.float32)
    half = QK_ROPE_DIM // 2
    x1, x2 = xf[..., :half], xf[..., half:]
    return jnp.concatenate([x1 * cos - x2 * sin, x2 * cos + x1 * sin], axis=-1).astype(x.dtype)

def mla_branch(c_q, c_kv, k_rope_raw, q_norm_g, kv_norm_g, w_uq, w_uk, w_uv, w_o_attn, cos, sin):
    B, S, _ = c_q.shape
    q = (rms_norm(c_q, q_norm_g) @ w_uq).reshape(B, S, N_HEADS, QK_DIM) * (QK_DIM ** -0.5)
    q_nope = q[..., :QK_NOPE_DIM]
    q_rope = apply_rope(q[..., QK_NOPE_DIM:], cos[None, :, None, :], sin[None, :, None, :])
    c = rms_norm(c_kv, kv_norm_g)
    k_nope = (c @ w_uk).reshape(B, S, N_HEADS, QK_NOPE_DIM)
    v = (c @ w_uv).reshape(B, S, N_HEADS, V_DIM)
    k_rope = apply_rope(k_rope_raw, cos[None], sin[None])
    nb = S // Q_BLOCK
    qn_blocks = q_nope.reshape(B, nb, Q_BLOCK, N_HEADS, QK_NOPE_DIM).transpose(1, 0, 2, 3, 4)
    qr_blocks = q_rope.reshape(B, nb, Q_BLOCK, N_HEADS, QK_ROPE_DIM).transpose(1, 0, 2, 3, 4)

    def attend(blk):
        qn, qr = blk
        s = (jnp.einsum('bqhd,bkhd->bhqk', qn, k_nope, preferred_element_type=jnp.float32)
             + jnp.einsum('bqhr,bkr->bhqk', qr, k_rope, preferred_element_type=jnp.float32))
        p = jax.nn.softmax(s, axis=-1).astype(v.dtype)
        return jnp.einsum('bhqk,bkhd->bqhd', p, v)

    o = lax.map(attend, (qn_blocks, qr_blocks))
    o = o.transpose(1, 0, 2, 3, 4).reshape(B, S, N_HEADS * V_DIM)
    return o @ w_o_attn

def fourier_branch(z, w_fourier):
    B, S, _ = z.shape
    zf = z.astype(jnp.float32).reshape(B, S, F_GROUPS, F_GROUP_DIM)
    y = jnp.fft.fft2(zf, axes=(1, 3), norm='ortho').real
    return y.astype(z.dtype).reshape(B, S, F_DIM) @ w_fourier

def peer(x, w_q, keys, w_u, w_v):
    B, S, D = x.shape
    T = B * S
    xt = x.reshape(T, D)
    q = (xt @ w_q).reshape(T, PEER_HEADS, 2, PEER_HALF)
    s_half = jnp.einsum('thcd,hcnd->thcn', q, keys, preferred_element_type=jnp.float32)
    sv, si = lax.top_k(s_half, PEER_TOPK)
    cand = (sv[:, :, 0, :, None] + sv[:, :, 1, None, :]).reshape(T, PEER_HEADS, PEER_TOPK * PEER_TOPK)
    cv, ci = lax.top_k(cand, PEER_TOPK)
    ia = jnp.take_along_axis(si[:, :, 0], ci // PEER_TOPK, axis=-1)
    ib = jnp.take_along_axis(si[:, :, 1], ci % PEER_TOPK, axis=-1)
    expert = (ia * PEER_NKEYS + ib).reshape(T, PEER_HEADS * PEER_TOPK)
    gate = jax.nn.softmax(cv, axis=-1).reshape(T, PEER_HEADS * PEER_TOPK)
    nc = T // PEER_CHUNK
    hk = PEER_HEADS * PEER_TOPK

    def run(blk):
        xc, ec, gc = blk
        u = jnp.take(w_u, ec, axis=0)
        h = jnp.einsum('cd,ced->ce', xc, u, preferred_element_type=jnp.float32)
        a = (jax.nn.gelu(h, approximate=False) * gc).astype(x.dtype)
        return jnp.einsum('ce,ced->cd', a, jnp.take(w_v, ec, axis=0))

    y = lax.map(run, (xt.reshape(nc, PEER_CHUNK, D), expert.reshape(nc, PEER_CHUNK, hk), gate.reshape(nc, PEER_CHUNK, hk)))
    return y.reshape(B, S, D)

def setup_inputs(seed: int = 0) -> dict:
    key = jax.random.key(seed)
    ks = jax.random.split(key, 24)
    f32 = jnp.float32

    def nrm(k, shape, scale):
        return jax.random.normal(k, shape, f32) * scale

    L = DEPTH
    return {
        'x': nrm(ks[0], (BATCH, SEQ, D_MODEL), 1.0),
        'ln0_g': 1.0 + nrm(ks[1], (D_MODEL,), 0.02),
        'ln0_b': nrm(ks[2], (D_MODEL,), 0.02),
        'w_in': nrm(ks[3], (L, D_MODEL, IN_DIM), D_MODEL ** -0.5),
        'b_in': nrm(ks[4], (L, IN_DIM), 0.02),
        'q_norm_g': 1.0 + nrm(ks[5], (L, Q_LORA), 0.02),
        'kv_norm_g': 1.0 + nrm(ks[6], (L, KV_LORA), 0.02),
        'w_uq': nrm(ks[7], (L, Q_LORA, N_HEADS * QK_DIM), Q_LORA ** -0.5),
        'w_uk': nrm(ks[8], (L, KV_LORA, N_HEADS * QK_NOPE_DIM), KV_LORA ** -0.5),
        'w_uv': nrm(ks[9], (L, KV_LORA, N_HEADS * V_DIM), DN_BETA * KV_LORA ** -0.5),
        'w_o_attn': nrm(ks[10], (L, N_HEADS * V_DIM, D_MODEL), (N_HEADS * V_DIM) ** -0.5),
        'w_fourier': nrm(ks[11], (L, F_DIM, D_MODEL), DN_BETA * F_DIM ** -0.5),
        'w_out': nrm(ks[12], (L, D_MODEL, D_MODEL), DN_BETA * D_MODEL ** -0.5),
        'b_out': nrm(ks[13], (L, D_MODEL), 0.02),
        'ln1_g': 1.0 + nrm(ks[14], (L, D_MODEL), 0.02),
        'ln1_b': nrm(ks[15], (L, D_MODEL), 0.02),
        'peer_w_q': nrm(ks[16], (L, D_MODEL, PEER_HEADS * PEER_QDIM), D_MODEL ** -0.5),
        'peer_keys': nrm(ks[17], (L, PEER_HEADS, 2, PEER_NKEYS, PEER_HALF), PEER_HALF ** -0.5),
        'peer_w_u': nrm(ks[18], (L, PEER_EXPERTS, D_MODEL), D_MODEL ** -0.5),
        'peer_w_v': nrm(ks[19], (L, PEER_EXPERTS, D_MODEL), DN_BETA),
        'ln2_g': 1.0 + nrm(ks[20], (L, D_MODEL), 0.02),
        'ln2_b': nrm(ks[21], (L, D_MODEL), 0.02),
    }

def reference(x, ln0_g, ln0_b, w_in, b_in, q_norm_g, kv_norm_g, w_uq, w_uk, w_uv, w_o_attn, w_fourier,
              w_out, b_out, ln1_g, ln1_b, peer_w_q, peer_keys, peer_w_u, peer_w_v, ln2_g, ln2_b):
    B, S, D = x.shape
    cos, sin = rotary_tables(S)
    h = layer_norm(x, ln0_g, ln0_b)
    for l in range(DEPTH):
        p = h @ w_in[l] + b_in[l]
        c_q, c_kv, k_r, z_f, g_logits = jnp.split(p, SPLITS, axis=-1)
        y_a = mla_branch(c_q, c_kv, k_r, q_norm_g[l], kv_norm_g[l], w_uq[l], w_uk[l], w_uv[l], w_o_attn[l], cos, sin)
        y_f = fourier_branch(z_f, w_fourier[l])
        g = jax.nn.sigmoid(g_logits.astype(jnp.float32)).astype(h.dtype).reshape(B, S, N_BRANCH, D)
        m = g[:, :, 0, :] * y_a + g[:, :, 1, :] * y_f
        h = layer_norm(DN_ALPHA * h + (m @ w_out[l] + b_out[l]), ln1_g[l], ln1_b[l])
        h = layer_norm(DN_ALPHA * h + peer(h, peer_w_q[l], peer_keys[l], peer_w_u[l], peer_w_v[l]), ln2_g[l], ln2_b[l])
    return h


_drawn_inputs = setup_inputs


def setup_inputs(seed=0):
    import zlib

    import numpy as np

    out = dict(_drawn_inputs(seed))
    spreads = {}
    factors = {'b_in': 3.416, 'q_norm_g': 8.0, 'kv_norm_g': 8.0, 'ln2_g': 2.958, 'ln2_b': 2.748}
    for name, (base, spread) in spreads.items():
        noise = np.random.default_rng([zlib.crc32(name.encode()), seed]).standard_normal(out[name].shape)
        drawn = base * np.exp(spread * noise) if base else spread * noise
        out[name] = __import__('jax').numpy.asarray(drawn.astype(out[name].dtype))
    for name, factor in factors.items():
        out[name] = (out[name] * factor).astype(out[name].dtype)
    return out
```

```python
import math
from contextlib import ExitStack

import concourse.bass as bass
import numpy as np
from concourse import mybir

D = 1024
S = 1024
H, NOPE, ROPE, VD = 8, 64, 32, 64
QK = NOPE + ROPE
LORA = 256
FG, FD = 4, 128
PH, NK, HALF, TOPK = 8, 128, 128, 16
P = 128
ALPHA = 2.0 ** 0.25
LN_EPS, RMS_EPS = 1e-5, 1e-6
KD = D // P
TT = S // P
TILES = 2
GROUP = TILES * P
GROUPS = S // GROUP
SLOTS = PH * TOPK
STEPS = TILES * SLOTS
BATCH = 8
AHEAD = 12
NU = NV = 4
NDIAG = 2 * BATCH
NW = 4
WQ0, WM0, WO0, WP0 = 0, 4, 4 + 3 * KD, 4 + 4 * KD
CHUNKS = WP0 + 2 * PH
NEG = -3.0e38

A0, A_PERIOD = 0, 4
M0, M_PERIOD = 72, 6
O0 = 120
L0 = 136
K0, K_PERIOD = 148, 4
T0 = K0 + 2 * K_PERIOD + 1
I0 = T0 + 2 * K_PERIOD * PH
HAND1 = SLOTS - AHEAD
HAND0 = STEPS - AHEAD
assert I0 + 8 * TILES <= HAND0


def layer_program(nc, x, lnp, w_lat, w_z, w_kr, b_lat, b_zT, b_krT, gqkv, w_uk, w_uv, b_gate, wstream,
                  peer_keys, peer_u, peer_v, ident_in, dft_seq, dft_ch, rope_tab, iota_in, out):
    fp32, i32, u32 = mybir.dt.float32, mybir.dt.int32, mybir.dt.uint32
    ALU, ACT, AX = mybir.AluOpType, mybir.ActivationFunctionType, mybir.AxisListType.X
    ctx = ExitStack()
    with ctx:
        def sb(name, shape, dt=fp32):
            return ctx.enter_context(nc.sbuf_tensor(name, shape, dt))

        def sem(name):
            return ctx.enter_context(nc.semaphore(name))

        hres_d = nc.dram_tensor("hres_spill", [S, D], fp32).ap()
        hT_d = nc.dram_tensor("hT_spill", [P, KD, S], fp32).ap()
        cqT_d = nc.dram_tensor("cqT_spill", [P, 2, S], fp32).ap()
        yT_d = nc.dram_tensor("yT_spill", [P, FG, S], fp32).ap()

        KT = sb("KT", [P, H, S])
        V = sb("V", [P, TT, H * VD])
        rows = sb("rows", [P, NU + NV, D])
        u_rows, v_rows = rows[:, 0:NU, :], rows[:, NU:NU + NV, :]
        wring = sb("wring", [P, NW, D])
        S2 = sb("S2", [P, TILES, 2 * PH, NK])
        hh = sb("hh", [P, 2 * TILES, D])
        h1_front, h1_peer = hh[:, 0:TILES, :], hh[:, TILES:2 * TILES, :]
        hT_g = sb("hT_g", [P, KD, GROUP])
        diag = sb("diag", [P, NDIAG, P])
        ln = sb("ln", [P, 4, D])
        keysT = sb("keysT", [P, 2 * PH, NK])
        yo = sb("yo", [P, 2, D])
        yT_g = yo[:, 0, :].rearrange("p (g t) -> p g t", g=FG)
        oT = yo[:, 1, :].rearrange("p (c t) -> p c t", c=4)
        cqT_g = sb("cqT_g", [P, 2, GROUP])
        o_sb = sb("o_sb", [P, H * VD])
        ybuf = sb("ybuf", [P, D])
        ident = sb("ident", [P, P])
        qcT = sb("qcT", [P, 2, GROUP])
        rope_g = sb("rope_g", [P, 2, GROUP])
        sg = sb("sg", [P, 2, GROUP])
        prod = sb("prod", [P, 2, GROUP])
        bg = sb("bg", [P, 2, KD])
        rowsum = sb("rowsum", [P, TILES, H])
        rrow = sb("rrow", [P, TILES, H])
        nmax = sb("nmax", [P, 2])
        sv = sb("sv", [P, TILES, 2 * PH, TOPK])
        si = sb("si", [P, TILES, 2 * PH, TOPK], u32)
        cv = sb("cv", [P, TILES, PH, TOPK])
        ci = sb("ci", [P, TILES, PH, TOPK], u32)
        cab = sb("cab", [P, 2, SLOTS])
        cabi = sb("cabi", [P, SLOTS], u32)
        iota16 = sb("iota16", [P, TOPK])
        gsum = sb("gsum", [P, PH])
        ids_front = sb("ids_front", [P, TILES, SLOTS], i32)
        ids_peer = sb("ids_peer", [P, TILES, SLOTS], i32)
        gate_front = sb("gate_front", [P, TILES, SLOTS])
        gate_peer = sb("gate_peer", [P, TILES, SLOTS])
        dots = sb("dots", [P, 2, BATCH])
        act_out = sb("act_out", [P, 2, BATCH])
        st = sb("st", [P, 3, 12])
        mv = sb("mv", [P, 3, 2])
        sd = sb("sd", [P, 3, 2])
        rq = sb("rq", [P, 4])
        gqk = sb("gqk", [P, 2, 2])
        bz = sb("bz", [P, FG])
        bkr = sb("bkr", [P, 2])
        s2_flat = S2[:, :, :, :].rearrange("p t c n -> p t (c n)")
        probs, probsT = s2_flat[:, 0, 0:S], s2_flat[:, 0, S:2 * S]
        mT = s2_flat[:, 1, :].rearrange("p (c t) -> p c t", c=KD)
        qT_g = hT_g
        onehot = hT_g[:, :, :].rearrange("p a b -> p (a b)").rearrange("p (s j) -> p s j", j=TOPK)

        hT_all = rows
        zcs = rows[:, :, :].rearrange("p t (g c) -> p t g c", g=FG)
        zT = hh
        w_lat_sb = S2[:, :, :, :].rearrange("p t c n -> p (t c n)").rearrange("p (k n) -> p k n", k=KD)
        w_z_sb = wring[:, :, :].rearrange("p a b -> p (a b)").rearrange("p (k n) -> p k n", k=KD)
        dft_ring = wring[:, :, :].rearrange("p r (m n) -> p r m n", m=2)
        w_kr_sb = diag[:, 0:4, :].rearrange("p a b -> p (a b)").rearrange("p (k n) -> p k n", k=KD)
        dftc = diag[:, 4:6, :].rearrange("p a b -> p (a b)")
        w_uk_sb = ln[:, 0, :].rearrange("p (k n) -> p k n", k=2)
        w_uv_sb = ln[:, 1, :].rearrange("p (k n) -> p k n", k=2)
        ln0 = KT[:, 0:3, :]
        h_t = KT[:, 3:5, :]
        hres_t = KT[:, 5:7, :]
        blat = KT[:, 7, 0:512]
        x_t = hT_g[:, :, :].rearrange("p a b -> p (a b)").rearrange("p (t d) -> p t d", t=2)
        c_t = V[:, 0:2, :]
        cqT_all = V[:, 4:8, :].rearrange("p a b -> p (a b)").rearrange("p (c t) -> p c t", c=2)
        ckvT_all = keysT[:, :, :].rearrange("p a b -> p (a b)").rearrange("p (c t) -> p c t", c=2)
        rope_all = yo
        keys_sb = hT_g[:, :, :].rearrange("p a b -> p (a b)").rearrange("p (c d) -> p c d", c=2 * PH)
        yT_half = S2[:, 0, :, :].rearrange("p a b -> p (a b)").rearrange("p (g t) -> p g t", g=FG)
        yT_half2 = S2[:, 1, :, :].rearrange("p a b -> p (a b)").rearrange("p (g t) -> p g t", g=FG)
        yT_halves = (yT_half, yT_half2)
        rope_tmp = prod[:, :, :].rearrange("p a b -> p (a b)")

        def ps(name, n):
            return ctx.enter_context(nc.psum_tensor(name, [P, n], fp32))

        acc = ps("acc", D)
        fA, fB = ps("fA", 1024), ps("fB", 1024)
        m0, m1 = ps("m0", 512), ps("m1", 512)
        banks = (fA[:, 0:512], fA[:, 512:1024], fB[:, 0:512], fB[:, 512:1024])

        consts_in, ln0_in = sem("consts_in"), sem("ln0_in")
        x_in = [sem(f"x_in{i}") for i in range(2)]
        w_lat_in, w_z_in, w_kv_in, rope_in, keys_in, ln_in = (
            sem(n) for n in ("w_lat_in", "w_z_in", "w_kv_in", "rope_in", "keys_in", "ln_in"))
        dft_in = [sem(f"dft_in{i}") for i in range(NW)]
        var0, std0, h0_done, h0T_ps, h0T_sb = (sem(n) for n in ("var0", "std0", "h0_done", "h0T_ps", "h0T_sb"))
        hres_out = [sem(f"hres_out{i}") for i in range(2)]
        lat_ps, lat_ms, lat_rms, lat_done, latT_ps, latT_sb = (
            sem(n) for n in ("lat_ps", "lat_ms", "lat_rms", "lat_done", "latT_ps", "latT_sb"))
        spilled = sem("spilled")
        z_ps, z_sb, kr_ps, kr_sb, kr_all = (sem(n) for n in ("z_ps", "z_sb", "kr_ps", "kr_sb", "kr_all"))
        k_ps, k_sb, v_ps, v_sb = (sem(n) for n in ("k_ps", "k_sb", "v_ps", "v_sb"))
        zc_ps, zc_sb, dft_used, y_half, y_half_sb = (
            sem(n) for n in ("zc_ps", "zc_sb", "dft_used", "y_half", "y_half_sb"))
        keys_ps, keys_sbuf = sem("keys_ps"), sem("keys_sbuf")
        q_in, hT_in, yT_in, hres_in = (sem(n) for n in ("q_in", "hT_in", "yT_in", "hres_in"))
        w_in_s = [sem(f"w_landed{i}") for i in range(NW)]
        w_free = sem("w_free")
        q_ps, q_nope, q_rope, scores_ps, row_max, probs_sb, probsT_ps, probsT_sb, pv_ps = (
            sem(n) for n in ("q_ps", "q_nope", "q_rope", "scores_ps", "row_max", "probs_sb", "probsT_ps",
                             "probsT_sb", "pv_ps"))
        o_done, oT_ps, oT_sb = (sem(n) for n in ("o_done", "oT_ps", "oT_sb"))
        gates_sb, m_done = sem("gates_sb"), sem("m_done")
        var1, std1, h1_done, h1T_ps, h1T_sb = (
            sem(n) for n in ("var1", "std1", "h1_done", "h1T_ps", "h1T_sb"))
        qc_sb, s_ps, s_sb = (sem(n) for n in ("qc_sb", "s_ps", "s_sb"))
        gmax_done, gexp_done = sem("gmax_done"), sem("gexp_done")
        handed = sem("handed")
        u_in = [sem(f"u_landed{i}") for i in range(NU)]
        v_in = [sem(f"v_landed{i}") for i in range(NV)]
        u_free, v_free, acc_free = sem("u_free"), sem("v_free"), sem("acc_free")
        act_done, diag_done = sem("act_done"), sem("diag_done")
        var2, std2, out_ready, out_stored = (sem(n) for n in ("var2", "std2", "out_ready", "out_stored"))

        block = ctx.enter_context(nc.Block())

        def tok(t):
            return slice(t * P, (t + 1) * P)

        def positive(v):
            return not isinstance(v, int) or v > 0

        def used(g, c):
            return g * CHUNKS + NW + c + 1

        @block.sync
        def _(sp):
            def load(dst, src, s):
                sp.dma_start(dst, src).then_inc(s, 16)

            load(ident[:, :], ident_in, consts_in)
            load(x_t[:, 0, :], x[tok(0), :], x_in[0])
            for j in range(3):
                load(ln0[:, j, :], lnp[j:j + 1, :].to_broadcast([P, D]), ln0_in)
            load(blat, b_lat[0:1, :].to_broadcast([P, 512]), ln0_in)
            load(w_lat_sb, w_lat, w_lat_in)
            load(x_t[:, 1, :], x[tok(1), :], x_in[1])
            for dst, src in ((gqk[:, :, :], gqkv), (bz[:, :], b_zT), (bkr[64:96, :], b_krT),
                             (bg[:, :, :], b_gate), (iota16[:, :], iota_in), (dftc, dft_ch)):
                load(dst, src, consts_in)
            load(w_z_sb, w_z, w_z_in)
            load(w_kr_sb, w_kr, w_z_in)
            load(w_uk_sb, w_uk, w_kv_in)
            load(w_uv_sb, w_uv, w_kv_in)
            load(rope_all[64:96, :, :], rope_tab, rope_in)
            for i in range(2, TT):
                sp.wait_ge(h0_done, i - 1)
                load(x_t[:, i % 2, :], x[tok(i), :], x_in[i % 2])
            for n in range(2 * TT):
                half, tt = divmod(n, TT)
                if n < NW:
                    sp.wait_ge(z_ps, 2 * FG)
                else:
                    sp.wait_ge(dft_used, n - NW + 1)
                load(dft_ring[:, n % NW, :, :],
                     dft_seq[:, tok(tt), half * 512:(half + 1) * 512].rearrange("m p n -> p m n"), dft_in[n % NW])
                if n == 3:
                    sp.wait_ge(h0_done, TT)
                    load(keys_sb, peer_keys.rearrange("c n d -> n c d"), keys_in)
            sp.wait_ge(k_ps, 2 * H)
            sp.wait_ge(v_ps, TT)
            for j in range(4):
                load(ln[:, j, :], lnp[3 + j:4 + j, :].to_broadcast([P, D]), ln_in)

            def stream(g):
                for c in range(CHUNKS):
                    sp.wait_ge(w_free, g * CHUNKS + c + 1)
                    n = 512 if c < WM0 else D
                    load(wring[:, c % NW, 0:n], wstream[c, :, 0:n], w_in_s[c % NW])

            sp.wait_ge(dft_used, 2 * TT)
            with sp.Fori(0, GROUPS) as g:
                stream(g)

        @block.gpsimd
        def _(pool):
            pool.wait_ge(kr_sb, 2)
            for h in range(1, H):
                nc.gpsimd.tensor_copy(KT[64:96, h, :], KT[64:96, 0, :]).then_inc(kr_all, 1)

            def gather_u(g, i):
                g, i = (g + 1, i - STEPS) if i >= STEPS else (g, i)
                if i % SLOTS == 0:
                    pool.wait_ge(handed, 2 * g + i // SLOTS + 1)
                pool.wait_ge(u_free, g * STEPS + i + 1)
                pool.nop(nofuse=True)
                t, s = divmod(i, SLOTS)
                pool.indirect_dma_start(
                    u_rows[:, i % NU, :], None, peer_u,
                    bass.IndirectOffsetOnAxis(ap=ids_peer[:, t, s:s + 1], axis=0)).then_inc(u_in[i % NU], 16)

            def gather_v(g, i):
                pool.wait_ge(v_free, g * STEPS + i + 1 + NDIAG - NV)
                pool.nop(nofuse=True)
                t, s = divmod(i, SLOTS)
                pool.indirect_dma_start(
                    v_rows[:, i % NV, :], None, peer_v,
                    bass.IndirectOffsetOnAxis(ap=ids_peer[:, t, s:s + 1], axis=0)).then_inc(v_in[i % NV], 16)

            def peer(g, last):
                for m in range(STEPS):
                    if m + AHEAD < STEPS or not last:
                        gather_u(g, m + AHEAD)
                    gather_v(g, m)

            for i in range(AHEAD):
                gather_u(0, i)
            with pool.Fori(0, GROUPS - 1) as g:
                peer(g, False)
            peer(GROUPS - 1, True)

        @block.tensor
        def _(pe):
            mm = nc.tensor.matmul

            def tr(out_, in_):
                return nc.tensor.transpose(out_, in_, ident[:, :])

            for _ in range(NDIAG):
                pe.nop().then_inc(v_free, 1)
            pe.wait_ge(consts_in, 16 * 7)
            for i in range(TT + 1):
                if i < TT:
                    pe.wait_ge(h0_done, i + 1)
                    if positive(i):
                        pe.wait_ge(h0T_sb, i)
                    for k in range(KD):
                        last = tr(fA[:, tok(k)], h_t[:, i % 2, tok(k)])
                    last.then_inc(h0T_ps, 1)
                if i >= 1:
                    j = i - 1
                    pe.wait_ge(lat_done, j + 1)
                    if positive(j):
                        pe.wait_ge(latT_sb, j)
                    for c in range(4):
                        last = tr(m1[:, tok(c)], c_t[:, j % 2, tok(c)])
                    last.then_inc(latT_ps, 1)
                if i < TT:
                    if i == 0:
                        pe.wait_ge(w_lat_in, 16)
                    pe.wait_ge(h0T_sb, i + 1)
                    if positive(i):
                        pe.wait_ge(lat_ms, i)
                    for k in range(KD):
                        last = mm(m0[:, :], hT_all[:, k, tok(i)], w_lat_sb[:, k, :], start=k == 0, stop=k == KD - 1)
                    last.then_inc(lat_ps, 1)
            pe.wait_ge(w_z_in, 32)
            for n in range(2 * FG):
                g, half = divmod(n, 2)
                if positive(n - 3):
                    pe.wait_ge(z_sb, n - 3)
                for k in range(KD):
                    last = mm(banks[n % 4], w_z_sb[:, k, g * FD:(g + 1) * FD], hT_all[:, k, half * 512:(half + 1) * 512],
                              start=k == 0, stop=k == KD - 1)
                last.then_inc(z_ps, 1)
            pe.wait_ge(latT_sb, TT)
            for half in range(2):
                for sw, bank in ((0, m0), (1, m1)):
                    if positive(half):
                        pe.wait_ge(kr_sb, half)
                    for k in range(KD):
                        last = mm(bank[64:96, :], w_kr_sb[:, k, sw * 32:(sw + 1) * 32],
                                  hT_all[:, k, half * 512:(half + 1) * 512], start=k == 0, stop=k == KD - 1)
                last.then_inc(kr_ps, 1)
            for n in range(TT * FG):
                tt, g = divmod(n, FG)
                if n == 0:
                    pe.wait_ge(hT_in, 16)
                if g == 0 or n == 0:
                    pe.wait_ge(z_sb, 2 * FG)
                if positive(n - 3):
                    pe.wait_ge(zc_sb, n - 3)
                mm(banks[n % 4][:, 0:2 * FD], zT[:, g, tok(tt)], dftc, start=True, stop=True).then_inc(zc_ps, 1)
            pe.wait_ge(w_kv_in, 32)
            pe.wait_ge(kr_sb, 2)
            for n in range(2 * H):
                h, half = divmod(n, 2)
                if positive(n - 1):
                    pe.wait_ge(k_sb, n - 1)
                for k in range(2):
                    last = mm((m0, m1)[n % 2][0:NOPE, :], w_uk_sb[:, k, h * NOPE:(h + 1) * NOPE],
                              ckvT_all[:, k, half * 512:(half + 1) * 512], start=k == 0, stop=k == 1)
                last.then_inc(k_ps, 1)
            pe.wait_ge(k_sb, 2 * H)
            for i in range(TT):
                if positive(i - 1):
                    pe.wait_ge(v_sb, i - 1)
                for k in range(2):
                    last = mm((m0, m1)[i % 2][:, :], ckvT_all[:, k, tok(i)], w_uv_sb[:, k, :], start=k == 0, stop=k == 1)
                last.then_inc(v_ps, 1)
            pe.wait_ge(zc_sb, TT * FG)
            for n in range(2 * TT):
                half, tt = divmod(n, TT)
                pe.wait_ge(dft_in[n % NW], 16 * (n // NW + 1))
                if tt == 0:
                    if positive(FG * half):
                        pe.wait_ge(y_half_sb, FG * half)
                for g in range(FG):
                    for cs in range(2):
                        last = mm(banks[g], zcs[:, tt, g, cs * FD:(cs + 1) * FD], dft_ring[:, n % NW, cs, :],
                                  start=tt == 0 and cs == 0, stop=tt == TT - 1 and cs == 1)
                last.then_inc(dft_used, 1)
            pe.wait_ge(keys_in, 16)
            pe.wait_ge(v_sb, TT)
            for b in range(4):
                if positive(b - 1):
                    pe.wait_ge(keys_sbuf, b - 1)
                for j in range(4):
                    last = tr((m0, m1)[b % 2][:, tok(j)], keys_sb[:, 4 * b + j, :])
                last.then_inc(keys_ps, 1)
            pe.wait_ge(keys_sbuf, 4)
            pe.wait_ge(y_half_sb, 2 * FG)
            for _ in range(NW):
                pe.nop().then_inc(w_free, 1)

            def chunk(g, c):
                pe.wait_ge(w_in_s[c % NW], g * (16 * CHUNKS // NW) + 16 * (c // NW + 1))
                return wring[:, c % NW, :]

            def front(g, m):
                for u in range(TILES * H):
                    a = A0 + A_PERIOD * u
                    qt, h = divmod(u, H)
                    if m == a and qt == 0:
                        c0 = WQ0 + 2 * (h // 4)
                        if h == 0:
                            pe.wait_ge(q_in, 32 * g + 32)
                        if h % 4 == 0:
                            chunk(g, c0)
                            chunk(g, c0 + 1)
                        if positive(g * H + h):
                            pe.wait_ge(q_nope, g * H + h)
                        if positive(g * H + h):
                            pe.wait_ge(q_rope, g * H + h)
                        if h == 0:
                            if positive(g * 2 * PH):
                                pe.wait_ge(s_sb, g * 2 * PH)
                        o = (h % 4) * P
                        for k in range(2):
                            last = mm(m0[0:QK, 0:GROUP], wring[:, (c0 + k) % NW, o:o + QK], cqT_g[:, k, :],
                                      start=k == 0, stop=k == 1)
                        for k in range(2):
                            last = mm(m0[64:96, GROUP:2 * GROUP], wring[:, (c0 + k) % NW, o + QK:o + P], cqT_g[:, k, :],
                                      start=k == 0, stop=k == 1)
                        last.then_inc(q_ps, 1)
                        if h % 4 == 3:
                            pe.drain().then_inc(w_free, 1)
                            pe.drain().then_inc(w_free, 1)
                    if m == a + 2:
                        if qt == 0:
                            pe.wait_ge(q_nope, g * H + h + 1)
                            pe.wait_ge(q_rope, g * H + h + 1)
                        if positive(g * TILES * H + u):
                            pe.wait_ge(probs_sb, g * TILES * H + u)
                        if u == 0:
                            if positive(g * TILES):
                                pe.wait_ge(h1T_sb, g * TILES)
                        for half in range(2):
                            last = mm(fA[:, half * 512:(half + 1) * 512], qT_g[0:QK, h, tok(qt)],
                                      KT[0:QK, h, half * 512:(half + 1) * 512], start=True, stop=True)
                        last.then_inc(scores_ps, 1)
                    if m == a + 5:
                        pe.wait_ge(probs_sb, g * TILES * H + u + 1)
                        if positive(g * TILES * H + u):
                            pe.wait_ge(probsT_sb, g * TILES * H + u)
                        for k in range(TT):
                            last = tr(fB[:, tok(k)], probs[:, tok(k)])
                        last.then_inc(probsT_ps, 1)
                    if m == a + 7:
                        pe.wait_ge(probsT_sb, g * TILES * H + u + 1)
                        if h == 0:
                            if positive(g * TILES + qt):
                                pe.wait_ge(o_done, g * TILES + qt)
                        for k in range(TT):
                            last = mm(m1[:, h * VD:(h + 1) * VD], probsT[:, tok(k)], V[:, k, h * VD:(h + 1) * VD],
                                      start=k == 0, stop=k == TT - 1)
                        last.then_inc(pv_ps, 1)
                    if h == H - 1 and m == a + 9:
                        pe.wait_ge(o_done, g * TILES + qt + 1)
                        if positive(g * TILES + qt):
                            pe.wait_ge(oT_sb, g * TILES + qt)
                        for c in range(4):
                            last = tr(m0[:, tok(c)], o_sb[:, tok(c)])
                        last.then_inc(oT_ps, 1)
                for dc in range(KD):
                    a = M0 + M_PERIOD * dc
                    gb, yb = banks[dc % 2], banks[2 + dc % 2]
                    for j in range(2):
                        if m == a + 2 * j:
                            if dc == 0 and j == 0:
                                pe.wait_ge(hT_in, 16 + 16 * (g + 1))
                                pe.wait_ge(probsT_sb, (g + 1) * TILES * H)
                            if j == 0:
                                if positive(g * KD + dc - 1):
                                    pe.wait_ge(gates_sb, g * KD + dc - 1)
                            w = chunk(g, WM0 + 3 * dc + j)
                            for k in range(KD):
                                last = mm(gb[:, j * GROUP:(j + 1) * GROUP], w[:, tok(k)], hT_g[:, k, :],
                                          start=k == 0, stop=k == KD - 1)
                            last.then_inc(w_free, 1)
                    if m == a + 4:
                        if dc == 0:
                            pe.wait_ge(yT_in, 16 * (g + 1))
                            pe.wait_ge(oT_sb, (g + 1) * TILES)
                        if positive(g * KD + dc - 1):
                            pe.wait_ge(m_done, g * KD + dc - 1)
                        w = chunk(g, WM0 + 3 * dc + 2)
                        for j, src in ((0, oT), (1, yT_g)):
                            for k in range(4):
                                last = mm(yb[:, j * GROUP:(j + 1) * GROUP], w[:, tok(4 * j + k)], src[:, k, :],
                                          start=k == 0, stop=k == 3)
                        last.then_inc(w_free, 1)
                for k in range(KD):
                    if m == O0 + 2 * k:
                        if k == 0:
                            pe.wait_ge(m_done, (g + 1) * KD)
                        w = chunk(g, WO0 + k)
                        for t in range(TILES):
                            for half in range(2):
                                last = mm(banks[2 * t + half], mT[:, k, tok(t)], w[:, half * 512:(half + 1) * 512],
                                          start=k == 0, stop=k == KD - 1)
                        last.then_inc(w_free, 1)
                for t in range(TILES):
                    if m == L0 + 4 + 4 * t:
                        pe.wait_ge(h1_done, g * TILES + t + 1)
                        for k in range(KD):
                            last = tr((fA, fB)[t][:, tok(k)], h1_front[:, t, tok(k)])
                        last.then_inc(h1T_ps, 1)
                for qc in range(2 * PH):
                    a = K0 + K_PERIOD * qc
                    if m == a:
                        if qc == 0:
                            pe.wait_ge(h1T_sb, (g + 1) * TILES)
                            pe.wait_ge(oT_sb, (g + 1) * TILES)
                        if positive(g * 2 * PH + qc - 1):
                            pe.wait_ge(qc_sb, g * 2 * PH + qc - 1)
                        w = chunk(g, WP0 + qc)
                        for k in range(KD):
                            last = mm(m0[:, (qc % 2) * GROUP:(qc % 2 + 1) * GROUP], w[:, tok(k)], hT_g[:, k, :],
                                      start=k == 0, stop=k == KD - 1)
                        last.then_inc(w_free, 1)
                    if m == a + 3:
                        pe.wait_ge(qc_sb, g * 2 * PH + qc + 1)
                        if positive(g * 2 * PH + qc - 1):
                            pe.wait_ge(s_sb, g * 2 * PH + qc - 1)
                        for t in range(TILES):
                            last = mm(m1[:, (qc % 2) * GROUP + t * P:(qc % 2) * GROUP + (t + 1) * P],
                                      qcT[:, qc % 2, tok(t)], keysT[:, qc, :], start=True, stop=True)
                        last.then_inc(s_ps, 1)

            def peer(g, i):
                if i % SLOTS == 0:
                    pe.wait_ge(acc_free, g * TILES + i // SLOTS + 1)
                if i % BATCH == 0:
                    pe.wait_ge(diag_done, g * STEPS + i + BATCH)
                pe.wait_ge(v_in[i % NV], g * (16 * STEPS // NV) + 16 * (i // NV + 1))
                for half in range(2):
                    last = mm(acc[:, half * 512:(half + 1) * 512], diag[:, i % NDIAG, :],
                              v_rows[:, i % NV, half * 512:(half + 1) * 512],
                              start=i % SLOTS == 0, stop=i % SLOTS == SLOTS - 1)
                last.then_inc(v_free, 1)

            for m in range(STEPS):
                front(0, m)
            with pe.Fori(0, GROUPS - 1) as g:
                for m in range(STEPS):
                    peer(g, m)
                    front(g + 1, m)
            for m in range(STEPS):
                peer(GROUPS - 1, m)

        @block.vector
        def _(dve):
            v = nc.vector

            def stats(n, src, var_ready):
                for half in range(2):
                    v.bn_stats(st[:, n, 6 * half:6 * half + 6], src[:, half * 512:(half + 1) * 512])
                dve.drain()
                v.bn_aggr(mv[:, n, :], st[:, n, :])
                dve.drain()
                v.tensor_scalar(sd[:, n, 0:1], mv[:, n, 1:2], LN_EPS, None, ALU.add).then_inc(var_ready, 1)

            def normalise(n, dst, src, std_ready, count, gamma, beta, done):
                dve.wait_ge(std_ready, count)
                v.reciprocal(sd[:, n, 0:1], sd[:, n, 1:2])
                dve.drain()
                v.tensor_scalar(dst, src, mv[:, n, 0:1], sd[:, n, 0:1], ALU.subtract, ALU.mult)
                dve.drain()
                v.tensor_tensor(dst, dst, gamma, ALU.mult)
                dve.drain()
                last = v.tensor_tensor(dst, dst, beta, ALU.add)
                if done is not None:
                    last.then_inc(done, 1)

            for _ in range(NU):
                dve.nop().then_inc(u_free, 1)
            dve.nop().then_inc(acc_free, 1)
            dve.wait_ge(ln0_in, 64)

            def latents(i):
                dve.wait_ge(lat_ps, i + 1)
                if positive(i - 1):
                    dve.wait_ge(latT_ps, i - 1)
                c = c_t[:, i % 2, :]
                v.tensor_tensor(c, m0[:, :], blat, ALU.add).then_inc(lat_ms, 1)
                dve.drain()
                for j in range(2):
                    v.tensor_tensor_reduce(out=ybuf[:, j * LORA:(j + 1) * LORA], in0=c[:, j * LORA:(j + 1) * LORA],
                                           in1=c[:, j * LORA:(j + 1) * LORA], scale=1.0, scalar=0.0,
                                           op0=ALU.mult, op1=ALU.add, accum_out=rq[:, j:j + 1])
                dve.drain()
                v.tensor_scalar(rq[:, 0:2], rq[:, 0:2], 1.0 / LORA, RMS_EPS, ALU.mult, ALU.add).then_inc(lat_rms, 1)
                dve.wait_ge(lat_rms, 2 * i + 2)
                v.reciprocal(rq[:, 0:2], rq[:, 2:4])
                dve.drain()
                v.tensor_scalar(c[:, 0:LORA], c[:, 0:LORA], rq[:, 0:1], None, ALU.mult)
                v.tensor_scalar(c[:, LORA:], c[:, LORA:], rq[:, 1:2], None, ALU.mult).then_inc(lat_done, 1)

            for i in range(TT):
                dve.wait_ge(x_in[i % 2], 16 * (i // 2 + 1))
                stats(0, x_t[:, i % 2, :], var0)
                if positive(i - 1):
                    dve.wait_ge(h0T_ps, i - 1)
                if i >= 2:
                    dve.wait_ge(hres_out[i % 2], 16 * (i // 2))
                normalise(0, h_t[:, i % 2, :], x_t[:, i % 2, :], std0, i + 1, ln0[:, 0, :], ln0[:, 1, :], None)
                dve.drain()
                v.scalar_tensor_tensor(out=hres_t[:, i % 2, :], in0=h_t[:, i % 2, :], scalar=ALPHA, in1=ln0[:, 2, :],
                                       op0=ALU.mult, op1=ALU.add).then_inc(h0_done, 1)
                if i >= 1:
                    latents(i - 1)
            latents(TT - 1)
            dve.wait_ge(rope_in, 16)
            dve.wait_ge(consts_in, 16 * 7)
            for i in range(2):
                dve.wait_ge(hres_out[i], 16 * (TT // 2))
            dve.wait_ge(h0T_ps, TT)
            for half in range(2):
                cols = slice(half * 512, (half + 1) * 512)
                dve.wait_ge(kr_ps, half + 1)
                v.scalar_tensor_tensor(out=rope_tmp[64:96, 0:512], in0=m0[64:96, :], scalar=bkr[64:96, 0:1],
                                       in1=rope_all[64:96, 0, cols], op0=ALU.add, op1=ALU.mult)
                v.scalar_tensor_tensor(out=ybuf[64:96, 0:512], in0=m1[64:96, :], scalar=bkr[64:96, 1:2],
                                       in1=rope_all[64:96, 1, cols], op0=ALU.add, op1=ALU.mult)
                dve.drain()
                v.tensor_tensor(KT[64:96, 0, cols], rope_tmp[64:96, 0:512], ybuf[64:96, 0:512],
                                ALU.add).then_inc(kr_sb, 1)
                dve.drain()
            for n in range(TT * FG):
                tt, g = divmod(n, FG)
                dve.wait_ge(zc_ps, n + 1)
                v.tensor_copy(zcs[:, tt, g, :], banks[n % 4][:, 0:2 * FD]).then_inc(zc_sb, 1)
            dve.wait_ge(spilled, 16)
            for i in range(TT):
                dve.wait_ge(v_ps, i + 1)
                v.tensor_copy(V[:, i, :], (m0, m1)[i % 2][:, :]).then_inc(v_sb, 1)
            for half in range(2):
                dve.wait_ge(dft_used, TT * (half + 1))
                for g in range(FG):
                    v.tensor_copy(yT_halves[half][:, g, :], banks[g]).then_inc(y_half_sb, 1)
            for b in range(4):
                dve.wait_ge(keys_ps, b + 1)
                v.tensor_copy(keysT[:, 4 * b:4 * b + 4, :].rearrange("p a b -> p (a b)"),
                              (m0, m1)[b % 2][:, :]).then_inc(keys_sbuf, 1)
            dve.wait_ge(ln_in, 64)
            dve.drain()

            def topk(vals, val16, idx16):
                v.max(val16[:, 0:8], vals)
                dve.drain()
                v.max_index(idx16[:, 0:8], val16[:, 0:8], vals)
                dve.drain()
                v.match_replace(vals, val16[:, 0:8], vals, NEG)
                dve.drain()
                v.max(val16[:, 8:16], vals)
                dve.drain()
                v.max_index(idx16[:, 8:16], val16[:, 8:16], vals)

            def front(g, m):
                for u in range(TILES * H):
                    a = A0 + A_PERIOD * u
                    qt, h = divmod(u, H)
                    if m == a and qt == 0:
                        dve.wait_ge(q_ps, g * H + h + 1)
                        if h == 0:
                            dve.wait_ge(q_in, 32 * g + 32)
                        v.tensor_tensor(prod[64:96, 0, :], m0[64:96, 0:GROUP], rope_g[64:96, 0, :], ALU.mult)
                        v.tensor_tensor(prod[64:96, 1, :], m0[64:96, GROUP:], rope_g[64:96, 1, :], ALU.mult)
                        dve.drain()
                        v.tensor_tensor(qT_g[64:96, h, :], prod[64:96, 0, :], prod[64:96, 1, :],
                                        ALU.add).then_inc(q_rope, 1)
                        dve.drain()
                    if m == a + 2:
                        dve.wait_ge(scores_ps, g * TILES * H + u + 1)
                        v.reduce_max(nmax[:, u % 2:u % 2 + 1], fA[:, :], AX)
                        dve.drain()
                        v.tensor_scalar(nmax[:, u % 2:u % 2 + 1], nmax[:, u % 2:u % 2 + 1], -(QK ** -0.5), None,
                                        ALU.mult).then_inc(row_max, 1)
                    if m == a + 5:
                        dve.wait_ge(probsT_ps, g * TILES * H + u + 1)
                        if positive(g * TILES * H + u):
                            dve.wait_ge(pv_ps, g * TILES * H + u)
                        v.tensor_copy(probsT, fB[:, :]).then_inc(probsT_sb, 1)
                    if h == H - 1 and m == a + 8:
                        dve.wait_ge(pv_ps, g * TILES * H + u + 1)
                        if positive(g * TILES + qt):
                            dve.wait_ge(oT_ps, g * TILES + qt)
                        v.reciprocal(rrow[:, qt, :], rowsum[:, qt, :])
                        dve.drain()
                        v.tensor_tensor(o_sb[:, :].rearrange("p (h d) -> p h d", h=H),
                                        m1[:, :].rearrange("p (h d) -> p h d", h=H),
                                        rrow[:, qt, :].unsqueeze(2).to_broadcast([P, H, VD]),
                                        ALU.mult).then_inc(o_done, 1)
                for dc in range(KD):
                    if m == M0 + M_PERIOD * dc + 5:
                        dve.wait_ge(gates_sb, g * KD + dc + 1)
                        dve.wait_ge(w_free, used(g, WM0 + 3 * dc + 2))
                        v.tensor_tensor(prod[:, :, :].rearrange("p a b -> p (a b)"),
                                        sg[:, :, :].rearrange("p a b -> p (a b)"), banks[2 + dc % 2], ALU.mult)
                        dve.drain()
                        v.tensor_tensor(mT[:, dc, :], prod[:, 0, :], prod[:, 1, :], ALU.add).then_inc(m_done, 1)
                        dve.drain()
                for t in range(TILES):
                    if m == L0 + 4 * t:
                        if t == 0:
                            dve.wait_ge(w_free, used(g, WP0 - 1))
                            dve.wait_ge(hres_in, 16 * (g + 1))
                        v.tensor_tensor(h1_front[:, t, :], h1_front[:, t, :], (fA, fB)[t][:, :], ALU.add)
                        dve.drain()
                        stats(1, h1_front[:, t, :], var1)
                    if m == L0 + 4 * t + 2:
                        normalise(1, h1_front[:, t, :], h1_front[:, t, :], std1, g * TILES + t + 1,
                                  ln[:, 0, :], ln[:, 1, :], h1_done)
                for h in range(PH):
                    for t in range(TILES):
                        a = T0 + 2 * K_PERIOD * h + 4 * t
                        for c in range(2):
                            if m == a + c:
                                if c == 0 and t == 0:
                                    dve.wait_ge(s_sb, g * 2 * PH + 2 * h + 2)
                                    dve.nop(nofuse=True)
                                topk(S2[:, t, 2 * h + c, :], sv[:, t, 2 * h + c, :], si[:, t, 2 * h + c, :])
                        if m == a + 2:
                            dve.drain()
                            cand = S2[:, t, 2 * h:2 * h + 2, :].rearrange("p a b -> p (a b)")
                            v.tensor_tensor(cand.rearrange("p (i j) -> p i j", i=TOPK),
                                            sv[:, t, 2 * h, :].unsqueeze(2).to_broadcast([P, TOPK, TOPK]),
                                            sv[:, t, 2 * h + 1, :].unsqueeze(1).to_broadcast([P, TOPK, TOPK]), ALU.add)
                            dve.drain()
                            topk(cand, cv[:, t, h, :], ci[:, t, h, :])
                for t in range(TILES):
                    a = I0 + 8 * t
                    flat_ci = ci[:, t, :, :].rearrange("p a b -> p (a b)")
                    if m == a:
                        dve.drain()
                        v.tensor_tensor(gate_front[:, t, :].rearrange("p (h k) -> p h k", h=PH), cv[:, t, :, :],
                                        cv[:, t, :, 0:1].to_broadcast([P, PH, TOPK]), ALU.subtract).then_inc(gmax_done, 1)
                        v.tensor_copy(sv[:, t, :, :], si[:, t, :, :])
                        v.tensor_single_scalar(cabi[:, :], flat_ci, 4, op=ALU.logical_shift_right)
                        dve.drain()
                        v.tensor_copy(cab[:, 0, :], cabi[:, :])
                        dve.drain()
                        v.tensor_single_scalar(cabi[:, :], flat_ci, 15, op=ALU.bitwise_and)
                        dve.drain()
                        v.tensor_copy(cab[:, 1, :], cabi[:, :])
                        dve.drain()
                    for c in range(2):
                        if m == a + 1 + 3 * c:
                            dve.drain()
                            v.tensor_tensor(onehot, cab[:, c, :].unsqueeze(2).to_broadcast([P, SLOTS, TOPK]),
                                            iota16[:, :].unsqueeze(1).to_broadcast([P, SLOTS, TOPK]), ALU.is_equal)
                        if m == a + 2 + 3 * c:
                            dve.drain()
                            for h in range(PH):
                                oh = onehot[:, h * TOPK:(h + 1) * TOPK, :]
                                v.tensor_tensor(oh, oh, sv[:, t, 2 * h + c, :].unsqueeze(1).to_broadcast([P, TOPK, TOPK]),
                                                ALU.mult)
                        if m == a + 3 + 3 * c:
                            dve.drain()
                            v.reduce_sum(cab[:, c, :], onehot, AX)
                    if m == a + 7:
                        dve.drain()
                        v.scalar_tensor_tensor(out=ids_front[:, t, :], in0=cab[:, 0, :], scalar=float(NK),
                                               in1=cab[:, 1, :], op0=ALU.mult, op1=ALU.add)
                        dve.wait_ge(gexp_done, g * TILES + t + 1)
                        gf = gate_front[:, t, :].rearrange("p (h k) -> p h k", h=PH)
                        v.reduce_sum(gsum[:, :], gf, AX)
                        dve.drain()
                        v.reciprocal(gsum[:, :], gsum[:, :])
                        dve.drain()
                        v.tensor_tensor(gf, gf, gsum[:, :].unsqueeze(2).to_broadcast([P, PH, TOPK]), ALU.mult)
                        dve.drain()

            def hand(t):
                dve.drain()
                v.tensor_copy(ids_peer[:, t, :], ids_front[:, t, :])
                v.tensor_copy(gate_peer[:, t, :], gate_front[:, t, :])
                v.tensor_copy(h1_peer[:, t, :], h1_front[:, t, :]).then_inc(handed, 1)
                dve.drain()

            def dot(g, i):
                g, i = (g + 1, i - STEPS) if i >= STEPS else (g, i)
                t = i // SLOTS
                dve.wait_ge(u_in[i % NU], g * (16 * STEPS // NU) + 16 * (i // NU + 1))
                row = u_rows[:, i % NU, :]
                b = i // BATCH % 2
                v.tensor_tensor_reduce(out=row, in0=row, in1=h1_peer[:, t, :], scale=1.0, scalar=0.0, op0=ALU.mult,
                                       op1=ALU.add, accum_out=dots[:, b, i % BATCH:i % BATCH + 1]).then_inc(u_free, 1)

            def diags(g, k):
                g, k = (g + 1, k - STEPS // BATCH) if k >= STEPS // BATCH else (g, k)
                dve.wait_ge(act_done, g * (STEPS // BATCH) + k + 1)
                dve.wait_ge(v_free, g * STEPS + BATCH * k + BATCH)
                t, s0 = divmod(k * BATCH, SLOTS)
                for s in range(BATCH):
                    v.tensor_scalar(diag[:, (k * BATCH + s) % NDIAG, :], ident[:, :], act_out[:, k % 2, s:s + 1],
                                    gate_peer[:, t, s0 + s:s0 + s + 1], ALU.mult, ALU.mult).then_inc(diag_done, 1)

            def finish(g, t):
                dve.wait_ge(v_free, g * STEPS + NDIAG + (t + 1) * SLOTS)
                v.scalar_tensor_tensor(out=ybuf[:, :], in0=h1_peer[:, t, :], scalar=ALPHA, in1=acc[:, :],
                                       op0=ALU.mult, op1=ALU.add).then_inc(acc_free, 1)
                dve.drain()
                stats(2, ybuf, var2)
                normalise(2, ybuf[:, :], ybuf[:, :], std2, g * TILES + t + 1, ln[:, 2, :], ln[:, 3, :], out_ready)
                dve.drain()

            def peer(g, m, last):
                if m == HAND1:
                    hand(1)
                if m == HAND0 and not last:
                    hand(0)
                if m + AHEAD < STEPS or not last:
                    dot(g, m + AHEAD)
                if m % BATCH == 5 and (m // BATCH + 1 < STEPS // BATCH or not last):
                    diags(g, m // BATCH + 1)
                if m % SLOTS == 6:
                    pass

            for m in range(STEPS):
                front(0, m)
            hand(0)
            for i in range(AHEAD):
                dot(0, i)
            diags(0, 0)

            def group(g, last):
                for m in range(STEPS):
                    peer(g, m, last)
                    if not last:
                        front(g + 1, m)
                    if m % SLOTS == SLOTS - 1:
                        finish(g, m // SLOTS)
                    if m % SLOTS == 8:
                        dve.wait_ge(out_stored, 16 * (g * TILES + m // SLOTS) + 16)

            with dve.Fori(0, GROUPS - 1) as g:
                group(g, False)
            group(GROUPS - 1, True)

        @block.scalar
        def _(act):
            s = nc.scalar

            act.wait_ge(consts_in, 16 * 7)

            def latent_cols(i):
                act.wait_ge(latT_ps, i + 1)
                for c in range(4):
                    dst = (cqT_all, ckvT_all)[c // 2][:, c % 2, tok(i)]
                    last = s.activation(dst, m1[:, tok(c)], ACT.Copy, scale=gqk[:, c // 2, c % 2:c % 2 + 1])
                last.then_inc(latT_sb, 1)

            for i in range(TT + 1):
                if i < TT:
                    act.wait_ge(var0, i + 1)
                    s.activation(sd[:, 0, 1:2], sd[:, 0, 0:1], ACT.Sqrt).then_inc(std0, 1)
                    act.wait_ge(h0_done, i + 1)
                    act.dma_start(hres_d[tok(i), :], hres_t[:, i % 2, :]).then_inc(hres_out[i % 2], 16)
                if i >= 1:
                    act.wait_ge(lat_rms, 2 * i - 1)
                    s.activation(rq[:, 2:4], rq[:, 0:2], ACT.Sqrt).then_inc(lat_rms, 1)
                if i < TT:
                    act.wait_ge(h0T_ps, i + 1)
                    s.activation(hT_all[:, :, tok(i)], fA[:, :].rearrange("p (k t) -> p k t", k=KD),
                                 ACT.Copy).then_inc(h0T_sb, 1)
                if i >= 1:
                    latent_cols(i - 1)
            act.drain()
            act.dma_start(hT_d, hT_all[:, :, :]).then_inc(hT_in, 16)
            act.dma_start(cqT_d, cqT_all).then_inc(spilled, 16)
            for n in range(2 * FG):
                g, half = divmod(n, 2)
                act.wait_ge(z_ps, n + 1)
                s.activation(zT[:, g, half * 512:(half + 1) * 512], banks[n % 4], ACT.Identity,
                             bias=bz[:, g:g + 1]).then_inc(z_sb, 1)
            act.wait_ge(kr_sb, 2)
            for n in range(2 * H):
                h, half = divmod(n, 2)
                act.wait_ge(k_ps, n + 1)
                s.activation(KT[0:NOPE, h, half * 512:(half + 1) * 512], (m0, m1)[n % 2][0:NOPE, :],
                             ACT.Copy).then_inc(k_sb, 1)
            act.wait_ge(y_half_sb, FG)
            act.dma_start(yT_d[:, :, 0:512], yT_half).then_inc(spilled, 16)
            act.wait_ge(y_half_sb, 2 * FG)
            act.dma_start(yT_d[:, :, 512:1024], yT_half2).then_inc(spilled, 16)
            act.wait_ge(spilled, 48)
            for i in range(2):
                act.wait_ge(hres_out[i], 16 * (TT // 2))
            act.wait_ge(hT_in, 16)
            act.wait_ge(kr_all, H - 1)
            act.dma_start(yo[0:1, 0, 0:P], hres_d[0:1, 0:P]).then_inc(out_stored, 16)
            act.wait_ge(out_stored, 16)

            def front(g, m):
                if m == 0:
                    if positive(2 * g - 1):
                        act.wait_ge(handed, 2 * g - 1)
                    act.dma_start(cqT_g[:, :, :], cqT_d[:, :, bass.ds(g * GROUP, GROUP)]).then_inc(q_in, 16)
                    act.dma_start(rope_g[64:96, :, :], rope_tab[:, :, bass.ds(g * GROUP, GROUP)]).then_inc(q_in, 16)
                    act.dma_start(yT_g, yT_d[:, :, bass.ds(g * GROUP, GROUP)]).then_inc(yT_in, 16)
                for u in range(TILES * H):
                    a = A0 + A_PERIOD * u
                    qt, h = divmod(u, H)
                    if m == a and qt == 0:
                        act.wait_ge(q_ps, g * H + h + 1)
                        s.activation(qT_g[0:NOPE, h, :], m0[0:NOPE, 0:GROUP], ACT.Copy).then_inc(q_nope, 1)
                    if m == a + 3:
                        act.wait_ge(row_max, g * TILES * H + u + 1)
                        if positive(g * TILES * H + u):
                            act.wait_ge(probsT_ps, g * TILES * H + u)
                        s.activation(probs, fA[:, :], ACT.Exp, bias=nmax[:, u % 2:u % 2 + 1], scale=QK ** -0.5,
                                     accum_out=rowsum[:, qt, h:h + 1]).then_inc(probs_sb, 1)
                    if h == H - 1 and m == a + 10:
                        act.wait_ge(oT_ps, g * TILES + qt + 1)
                        s.activation(oT[:, :, tok(qt)], m0[:, :].rearrange("p (c t) -> p c t", c=4),
                                     ACT.Copy).then_inc(oT_sb, 1)
                if m == A0 + A_PERIOD * (TILES * H - 1) + 3:
                    act.wait_ge(scores_ps, (g + 1) * TILES * H)
                    act.dma_start(hT_g[:, :, :], hT_d[:, :, bass.ds(g * GROUP, GROUP)]).then_inc(hT_in, 16)
                for dc in range(KD):
                    if m == M0 + M_PERIOD * dc + 3:
                        act.wait_ge(w_free, used(g, WM0 + 3 * dc + 1))
                        if positive(g * KD + dc):
                            act.wait_ge(m_done, g * KD + dc)
                        for j in range(2):
                            last = s.activation(sg[:, j, :], banks[dc % 2][:, j * GROUP:(j + 1) * GROUP], ACT.Sigmoid,
                                                bias=bg[:, j, dc:dc + 1])
                        last.then_inc(gates_sb, 1)
                if m == HAND1 + 2:
                    if positive(2 * g):
                        act.wait_ge(handed, 2 * g)
                    act.dma_start(h1_front, hres_d[bass.ds(g * GROUP, GROUP), :].rearrange("(t p) d -> p t d", p=P)
                                  ).then_inc(hres_in, 16)
                for t in range(TILES):
                    if m == L0 + 4 * t + 1:
                        act.wait_ge(var1, g * TILES + t + 1)
                        s.activation(sd[:, 1, 1:2], sd[:, 1, 0:1], ACT.Sqrt).then_inc(std1, 1)
                    if m == L0 + 4 * t + 6:
                        act.wait_ge(h1T_ps, g * TILES + t + 1)
                        s.activation(hT_g[:, :, tok(t)], (fA, fB)[t][:, :].rearrange("p (k t) -> p k t", k=KD),
                                     ACT.Copy).then_inc(h1T_sb, 1)
                for qc in range(2 * PH):
                    a = K0 + K_PERIOD * qc
                    if m == a + 1:
                        act.wait_ge(w_free, used(g, WP0 + qc))
                        if positive(g * 2 * PH + qc - 1):
                            act.wait_ge(s_ps, g * 2 * PH + qc - 1)
                        s.activation(qcT[:, qc % 2, :], m0[:, (qc % 2) * GROUP:(qc % 2 + 1) * GROUP],
                                     ACT.Copy).then_inc(qc_sb, 1)
                    if m == a + 4:
                        act.wait_ge(s_ps, g * 2 * PH + qc + 1)
                        s.activation(S2[:, :, qc, :],
                                     m1[:, (qc % 2) * GROUP:(qc % 2 + 1) * GROUP].rearrange("p (t n) -> p t n", t=TILES),
                                     ACT.Copy).then_inc(s_sb, 1)
                for t in range(TILES):
                    if m == I0 + 8 * t + 2:
                        act.wait_ge(gmax_done, g * TILES + t + 1)
                        s.activation(gate_front[:, t, :], gate_front[:, t, :], ACT.Exp).then_inc(gexp_done, 1)

            def gelu(g, k):
                g, k = (g + 1, k - STEPS // BATCH) if k >= STEPS // BATCH else (g, k)
                act.wait_ge(u_free, g * STEPS + NU + BATCH * (k + 1))
                s.activation(act_out[:, k % 2, :], dots[:, k % 2, :], ACT.Gelu).then_inc(act_done, 1)

            def finish(g, t):
                act.wait_ge(var2, g * TILES + t + 1)
                s.activation(sd[:, 2, 1:2], sd[:, 2, 0:1], ACT.Sqrt).then_inc(std2, 1)
                act.wait_ge(out_ready, g * TILES + t + 1)
                act.dma_start(out[bass.ds(g * GROUP + t * P, P), :], ybuf[:, :]).then_inc(out_stored, 16)

            for m in range(STEPS):
                front(0, m)
            gelu(0, 0)

            def group(g, last):
                for m in range(STEPS):
                    if m % BATCH == 4 and (m // BATCH + 1 < STEPS // BATCH or not last):
                        gelu(g, m // BATCH + 1)
                    if not last:
                        front(g + 1, m)
                    if m % SLOTS == SLOTS - 1:
                        finish(g, m // SLOTS)

            with act.Fori(0, GROUPS - 1) as g:
                group(g, False)
            group(GROUPS - 1, True)
            act.wait_ge(out_stored, 16 * (TT + 1))


def kernel(**inputs):
    from concourse import bacc
    from concourse.bass_utils import run_bass_kernel_spmd

    f = {n: np.asarray(a) for n, a in inputs.items()}
    w_in, b_in = f["w_in"][0], f["b_in"][0]
    kr0, z0, g0 = 2 * LORA, 2 * LORA + ROPE, 2 * LORA + ROPE + FG * FD

    def blocks(w):
        return np.ascontiguousarray(w.reshape(-1, P, w.shape[-1]).transpose(1, 0, 2))

    swap = np.r_[ROPE // 2:ROPE, 0:ROPE // 2]
    w_kr = w_in[:, kr0:z0]
    b_kr = b_in[kr0:z0]
    uq = f["w_uq"][0].reshape(2, P, H, QK)
    uq = np.concatenate([uq, uq[..., NOPE + swap]], axis=-1)
    chunks = []
    for half in range(2):
        for k in range(2):
            c = uq[k, :, 4 * half:4 * half + 4].reshape(P, 512)
            chunks.append(np.concatenate([c, c], axis=1))
    wo, wf = blocks(f["w_o_attn"][0]), blocks(f["w_fourier"][0])
    gw = blocks(w_in[:, g0:])
    for dc in range(KD):
        cols = slice(dc * P, (dc + 1) * P)
        for j in range(2):
            chunks.append(gw[:, :, j * D + dc * P:j * D + (dc + 1) * P].reshape(P, D))
        chunks.append(np.concatenate([wo[:, :, cols], wf[:, :, cols]], axis=1).reshape(P, D))
    chunks += list(f["w_out"][0].reshape(KD, P, D))
    wq = blocks(f["peer_w_q"][0])
    for qc in range(2 * PH):
        chunks.append(wq[:, :, qc * P:(qc + 1) * P].reshape(P, D))

    pos = np.arange(S, dtype=np.float32)
    inv = (1.0 / (np.float32(10000.0) ** (np.arange(0, ROPE, 2, dtype=np.float32) / ROPE))).astype(np.float32)
    ang = (pos[None, :] * inv[:, None]).astype(np.float32)
    cos, sin = np.cos(ang), np.sin(ang)
    rope = np.stack([np.concatenate([cos, cos]), np.concatenate([-sin, sin])], axis=1).astype(np.float32)
    n = np.arange(S)
    w = 2 * math.pi * ((n[:, None] * n[None, :]) % S) / S
    dft_seq = np.stack([np.cos(w), np.sin(w)]).astype(np.float32)
    c = np.arange(FD)
    w = 2 * math.pi * ((c[:, None] * c[None, :]) % FD) / FD
    dft_ch = (np.concatenate([np.cos(w), -np.sin(w)], axis=1) / math.sqrt(S * FD)).astype(np.float32)

    arrays = {
        "x": f["x"][0],
        "lnp": np.stack([f["ln0_g"], f["ln0_b"], f["b_out"][0], f["ln1_g"][0], f["ln1_b"][0],
                         f["ln2_g"][0], f["ln2_b"][0]]),
        "w_lat": blocks(w_in[:, :kr0]),
        "w_z": blocks(w_in[:, z0:g0]),
        "w_kr": blocks(np.concatenate([w_kr, w_kr[:, swap]], axis=1)),
        "b_lat": b_in[None, :kr0],
        "b_zT": b_in[z0:g0].reshape(FG, FD).T,
        "b_krT": np.stack([b_kr, b_kr[swap]], axis=1),
        "gqkv": np.stack([f["q_norm_g"][0].reshape(2, P), f["kv_norm_g"][0].reshape(2, P)]).transpose(2, 0, 1),
        "w_uk": blocks(f["w_uk"][0]),
        "w_uv": blocks(f["w_uv"][0]),
        "b_gate": b_in[g0:].reshape(2, KD, P).transpose(2, 0, 1),
        "wstream": np.stack(chunks),
        "peer_keys": f["peer_keys"][0].reshape(2 * PH, NK, HALF),
        "peer_u": f["peer_w_u"][0],
        "peer_v": f["peer_w_v"][0],
        "ident_in": np.eye(P, dtype=np.float32),
        "dft_seq": dft_seq,
        "dft_ch": dft_ch,
        "rope_tab": rope,
        "iota_in": np.tile(np.arange(TOPK, dtype=np.float32), (P, 1)),
    }
    nc = bacc.Bacc("TRN2", target_bir_lowering=False, num_devices=1)
    args, feeds = [], {}
    for name, a in arrays.items():
        a = np.ascontiguousarray(a)
        feeds[f"in_{name}"] = a
        args.append(nc.dram_tensor(f"in_{name}", a.shape, mybir.dt.from_np(a.dtype), kind="ExternalInput").ap())
    args.append(nc.dram_tensor("out_h", (S, D), mybir.dt.float32, kind="ExternalOutput").ap())
    layer_program(nc, *args)
    r = run_bass_kernel_spmd(nc, [feeds], core_ids=[0])
    return r.results[0]["out_h"].reshape(1, S, D)
```

```python
import math
from contextlib import ExitStack

import concourse.bass as bass
import numpy as np
from concourse import mybir

D = 1024
S = 1024
H, NOPE, ROPE, VD = 8, 64, 32, 64
QK = NOPE + ROPE
LORA = 256
FG, FD = 4, 128
PH, NK, HALF, TOPK = 8, 128, 128, 16
P = 128
ALPHA = 2.0 ** 0.25
LN_EPS, RMS_EPS = 1e-5, 1e-6
KD = D // P
TT = S // P
TILES = 2
GROUP = TILES * P
GROUPS = S // GROUP
SLOTS = PH * TOPK
STEPS = TILES * SLOTS
BATCH = 8
AHEAD = 12
LEAD = 64
PAIRS = PH // 2
PSLOTS = SLOTS // PAIRS
NU = NV = 4
NDIAG = 2 * BATCH
NW = 4
NDFT = 4
WQ0, WM0, WO0, WP0 = 0, 4, 4 + 3 * KD, 4 + 4 * KD
CHUNKS = WP0 + 2 * PH
NEG = -3.0e38

A0, A_PERIOD = 0, 4
M0, M_PERIOD = 72, 6
O0 = 120
L0 = 136
K0, K_PERIOD = 148, 4
T0, T_PERIOD = K0 + 2 * K_PERIOD + 1, 2 * K_PERIOD
R0, R_PERIOD = 27, 12
IDS = 3
HAND1 = SLOTS - AHEAD - LEAD
HAND0 = STEPS - AHEAD - LEAD
assert T0 + T_PERIOD + IDS + 3 < HAND0 and T_PERIOD <= PSLOTS // 2 and T0 + PH * T_PERIOD <= STEPS
assert R0 + R_PERIOD + IDS + 3 < HAND1 and R_PERIOD <= PSLOTS // 2 and R0 + PH * R_PERIOD < K0
assert LEAD % BATCH == 0


def layer_program(nc, x, lnp, w_lat, w_z, w_kr, b_lat, b_zT, b_krT, gqkv, w_uk, w_uv, b_gate, wstream,
                  peer_keys, peer_u, peer_v, ident_in, dft_seq, dft_ch, rope_tab, iota_in, altern_in, out):
    fp32, i32, u32 = mybir.dt.float32, mybir.dt.int32, mybir.dt.uint32
    ALU, ACT, AX = mybir.AluOpType, mybir.ActivationFunctionType, mybir.AxisListType.X
    ctx = ExitStack()
    with ctx:
        def sb(name, shape, dt=fp32):
            return ctx.enter_context(nc.sbuf_tensor(name, shape, dt))

        def sem(name):
            return ctx.enter_context(nc.semaphore(name))

        hres_d = nc.dram_tensor("hres_spill", [S, D], fp32).ap()
        hT_d = nc.dram_tensor("hT_spill", [P, KD, S], fp32).ap()
        cqT_d = nc.dram_tensor("cqT_spill", [P, 2, S], fp32).ap()
        yT_d = nc.dram_tensor("yT_spill", [P, FG, S], fp32).ap()

        KT = sb("KT", [P, H, S])
        V = sb("V", [P, TT, H * VD])
        rows = sb("rows", [P, NU + NV, D])
        u_rows, v_rows = rows[:, 0:NU, :], rows[:, NU:NU + NV, :]
        wring = sb("wring", [P, NW, D])
        S2 = sb("S2", [P, TILES, 2 * PH, NK])
        hh = sb("hh", [P, 2 * TILES, D])
        h1_front, h1_peer = hh[:, 0:TILES, :], hh[:, TILES:2 * TILES, :]
        hT_g = sb("hT_g", [P, KD, GROUP])
        diag = sb("diag", [P, NDIAG, P])
        ln = sb("ln", [P, 4, D])
        keysT = sb("keysT", [P, 2 * PH, NK])
        yo = sb("yo", [P, 2, D])
        yT_g = yo[:, 0, :].rearrange("p (g t) -> p g t", g=FG)
        oT = yo[:, 1, :].rearrange("p (c t) -> p c t", c=4)
        cqT_g = sb("cqT_g", [P, 2, GROUP])
        o_sb = sb("o_sb", [P, H * VD])
        ybuf = sb("ybuf", [P, D])
        ident = sb("ident", [P, P])
        qcT = sb("qcT", [P, 2, GROUP])
        rope_g = sb("rope_g", [P, GROUP])
        sg = sb("sg", [P, 2, GROUP])
        prod = sb("prod", [P, 2, GROUP])
        bg = sb("bg", [P, 2, KD])
        rowsum = sb("rowsum", [P, TILES, H])
        rrow = sb("rrow", [P, TILES, H])
        nmax = sb("nmax", [P, 2])
        sv = sb("sv", [P, TILES, 2 * PH, TOPK])
        si = sb("si", [P, TILES, 2 * PH, TOPK], u32)
        cv = sb("cv", [P, TILES, PH, TOPK])
        ci = sb("ci", [P, TILES, PH, TOPK], u32)
        cab = sb("cab", [P, 2, PSLOTS])
        cabi = sb("cabi", [P, 2, PSLOTS], u32)
        iota16 = sb("iota16", [P, TOPK])
        altern = sb("altern", [P, 1])
        ymid = sb("ymid", [P, FG])
        gsum = sb("gsum", [P, 2])
        ids_peer = sb("ids_peer", [P, TILES, SLOTS], i32)
        gate_front = sb("gate_front", [P, TILES, SLOTS])
        gate_peer = sb("gate_peer", [P, TILES, SLOTS])
        dots = sb("dots", [P, 2, BATCH])
        act_out = sb("act_out", [P, 2, BATCH])
        st = sb("st", [P, 3, 12])
        mv = sb("mv", [P, 3, 2])
        sd = sb("sd", [P, 3, 2])
        rq = sb("rq", [P, 4])
        gqk = sb("gqk", [P, 2, 2])
        bz = sb("bz", [P, FG])
        bkr = sb("bkr", [P, 1])
        s2_flat = S2[:, :, :, :].rearrange("p t c n -> p t (c n)")
        probs, probsT = s2_flat[:, 0, 0:S], s2_flat[:, 0, S:2 * S]
        mT = s2_flat[:, 0, :].rearrange("p (c t) -> p c t", c=KD)
        qT_g = hT_g
        onehot = sb("onehot", [P, PSLOTS, TOPK])

        hT_all = rows
        zcs = rows[:, :, :].rearrange("p t (g c) -> p t g c", g=FG)
        zT = hh
        w_lat_sb = S2[:, :, :, :].rearrange("p t c n -> p (t c n)").rearrange("p (k n) -> p k n", k=KD)
        w_z_sb = wring[:, :, :].rearrange("p a b -> p (a b)").rearrange("p (k n) -> p k n", k=KD)
        dft_ring = ln[:, :, :].rearrange("p r (m n) -> p r m n", m=2)
        w_kr_sb = diag[:, 0:4, :].rearrange("p a b -> p (a b)").rearrange("p (k n) -> p k n", k=KD)
        dftc = diag[:, 4:6, :].rearrange("p a b -> p (a b)")
        w_uk_sb = ln[:, 0, :].rearrange("p (k n) -> p k n", k=2)
        w_uv_sb = ln[:, 1, :].rearrange("p (k n) -> p k n", k=2)
        ln0 = KT[:, 0:3, :]
        h_t = KT[:, 3:5, :]
        hres_t = KT[:, 5:7, :]
        blat = KT[:, 7, 0:512]
        x_t = hT_g[:, :, :].rearrange("p a b -> p (a b)").rearrange("p (t d) -> p t d", t=2)
        c_t = V[:, 0:2, :]
        cqT_all = V[:, 4:8, :].rearrange("p a b -> p (a b)").rearrange("p (c t) -> p c t", c=2)
        ckvT_all = keysT[:, :, :].rearrange("p a b -> p (a b)").rearrange("p (c t) -> p c t", c=2)
        rope_all = yo[:, 0, :]
        keys_sb = hT_g[:, :, :].rearrange("p a b -> p (a b)").rearrange("p (c d) -> p c d", c=2 * PH)
        y_part = h1_peer
        rope_tmp = prod[:, :, :].rearrange("p a b -> p (a b)")
        zsum = rope_tmp.rearrange("p (g c) -> p g c", g=FG)

        def ps(name, n):
            return ctx.enter_context(nc.psum_tensor(name, [P, n], fp32))

        acc = ps("acc", D)
        fA, fB = ps("fA", 1024), ps("fB", 1024)
        m0, m1 = ps("m0", 512), ps("m1", 512)
        banks = (fA[:, 0:512], fA[:, 512:1024], fB[:, 0:512], fB[:, 512:1024])

        cos_part, sin_part = acc[:, 0:512], acc[:, 512:1024]

        consts_in, ln0_in = sem("consts_in"), sem("ln0_in")
        x_in = [sem(f"x_in{i}") for i in range(2)]
        w_lat_in, w_z_in, w_kv_in, rope_in, keys_in, ln_in = (
            sem(n) for n in ("w_lat_in", "w_z_in", "w_kv_in", "rope_in", "keys_in", "ln_in"))
        dft_in = [sem(f"dft_in{i}") for i in range(NDFT)]
        var0, std0, h0_done, hres_made, hres_sum, h0T_ps, h0T_sb = (sem(n) for n in ("var0", "std0", "h0_done", "hres_made", "hres_sum", "h0T_ps", "h0T_sb"))
        hres_out = [sem(f"hres_out{i}") for i in range(2)]
        lat_ps, lat_ms, lat_rms, lat_done, latT_ps, latT_sb = (
            sem(n) for n in ("lat_ps", "lat_ms", "lat_rms", "lat_done", "latT_ps", "latT_sb"))
        z_ps, z_sb, kr_ps, kr_sb, kr_all = (sem(n) for n in ("z_ps", "z_sb", "kr_ps", "kr_sb", "kr_all"))
        k_ps, k_sb, v_ps, v_sb = (sem(n) for n in ("k_ps", "k_sb", "v_ps", "v_sb"))
        zc_ps, dft_used, y_mid, y_done = (sem(n) for n in ("zc_ps", "dft_used", "y_mid", "y_done"))
        z_sum = sem("z_sum")
        zc_sb = [sem(f"zc_sb{i}") for i in range(2)]
        y_spilled = [sem(f"y_spilled{i}") for i in range(2)]
        keys_ps, keys_sbuf = sem("keys_ps"), sem("keys_sbuf")
        q_in, hT_in, yT_in, hres_in = (sem(n) for n in ("q_in", "hT_in", "yT_in", "hres_in"))
        w_in_s = [sem(f"w_landed{i}") for i in range(NW)]
        w_free = sem("w_free")
        q_ps, q_nope, q_rope, scores_ps, row_max, probs_sb, probsT_ps, probsT_sb, pv_ps = (
            sem(n) for n in ("q_ps", "q_nope", "q_rope", "scores_ps", "row_max", "probs_sb", "probsT_ps",
                             "probsT_sb", "pv_ps"))
        o_done, oT_ps, oT_sb = (sem(n) for n in ("o_done", "oT_ps", "oT_sb"))
        gates_sb, m_done = sem("gates_sb"), sem("m_done")
        var1, std1, h1_done, h1T_ps, h1T_sb = (
            sem(n) for n in ("var1", "std1", "h1_done", "h1T_ps", "h1T_sb"))
        qc_sb, s_ps, s_sb = (sem(n) for n in ("qc_sb", "s_ps", "s_sb"))
        gmax_done, gexp_done = sem("gmax_done"), sem("gexp_done")
        handed, h1_handed = sem("handed"), sem("h1_handed")
        u_in = [sem(f"u_landed{i}") for i in range(NU)]
        v_in = [sem(f"v_landed{i}") for i in range(NV)]
        u_free, v_free, acc_free = sem("u_free"), sem("v_free"), sem("acc_free")
        act_done, diag_done = sem("act_done"), sem("diag_done")
        var2, std2, out_ready, stored = (sem(n) for n in ("var2", "std2", "out_ready", "stored"))

        block = ctx.enter_context(nc.Block())

        def tok(t):
            return slice(t * P, (t + 1) * P)

        def positive(v):
            return not isinstance(v, int) or v > 0

        def slot_of(g, i):
            return (g + 1, i - STEPS) if i >= STEPS else (g, i)

        def has_slot(g, i, last):
            return i < STEPS and not (isinstance(g, int) and g < 0) or i >= STEPS and not last

        def used(g, c):
            return g * CHUNKS + NW + c + 1

        @block.sync
        def _(sp):
            def load(dst, src, s):
                sp.dma_start(dst, src).then_inc(s, 16)

            load(ident[:, :], ident_in, consts_in)
            load(x_t[:, 0, :], x[tok(0), :], x_in[0])
            for j in range(3):
                load(ln0[:, j, :], lnp[j:j + 1, :].to_broadcast([P, D]), ln0_in)
            load(blat, b_lat[0:1, :].to_broadcast([P, 512]), ln0_in)
            load(w_lat_sb, w_lat, w_lat_in)
            load(x_t[:, 1, :], x[tok(1), :], x_in[1])
            for dst, src in ((gqk[:, :, :], gqkv), (bz[:, :], b_zT), (bkr[64:128, :], b_krT),
                             (bg[:, :, :], b_gate), (iota16[:, :], iota_in), (dftc, dft_ch), (altern[:, :], altern_in)):
                load(dst, src, consts_in)
            load(w_z_sb, w_z, w_z_in)
            load(w_kr_sb, w_kr, w_z_in)
            load(w_uk_sb, w_uk, w_kv_in)
            load(w_uv_sb, w_uv, w_kv_in)
            load(rope_all[64:128, :], rope_tab, rope_in)
            for i in range(2, TT):
                sp.wait_ge(h0_done, i - 1)
                load(x_t[:, i % 2, :], x[tok(i), :], x_in[i % 2])
            sp.wait_ge(h0_done, TT)
            load(keys_sb, peer_keys.rearrange("c n d -> n c d"), keys_in)

            def stream(g):
                for c in range(CHUNKS):
                    sp.wait_ge(w_free, g * CHUNKS + c + 1)
                    n = 512 if c < WM0 else D
                    load(wring[:, c % NW, 0:n], wstream[c, :, 0:n], w_in_s[c % NW])

            sp.wait_ge(z_ps, 2 * FG)
            with sp.Fori(0, GROUPS) as g:
                stream(g)

        @block.gpsimd
        def _(pool):
            pool.wait_ge(ln0_in, 64)
            for i in range(TT):
                pool.wait_ge(h0_done, i + 1)
                if i >= 2:
                    pool.wait_ge(hres_out[i % 2], 16 * (i // 2))
                nc.gpsimd.tensor_scalar(hres_t[:, i % 2, :], h_t[:, i % 2, :], ALPHA, None, ALU.mult).then_inc(hres_made, 1)
                pool.wait_ge(hres_made, i + 1)
                nc.gpsimd.tensor_tensor(hres_t[:, i % 2, :], hres_t[:, i % 2, :], ln0[:, 2, :], ALU.add).then_inc(hres_sum, 1)
            pool.wait_ge(kr_sb, 2)
            for h in range(1, H):
                nc.gpsimd.tensor_copy(KT[64:96, h, :], KT[64:96, 0, :]).then_inc(kr_all, 1)
            def gather_u(g, i):
                g, i = slot_of(g, i)
                if i % PSLOTS == 0:
                    pool.wait_ge(handed, g * TILES * PAIRS + i // PSLOTS + 1)
                pool.wait_ge(u_free, g * STEPS + i + 1)
                pool.nop(nofuse=True)
                t, s = divmod(i, SLOTS)
                pool.indirect_dma_start(
                    u_rows[:, i % NU, :], None, peer_u,
                    bass.IndirectOffsetOnAxis(ap=ids_peer[:, t, s:s + 1], axis=0)).then_inc(u_in[i % NU], 16)

            def gather_v(g, i):
                g, i = slot_of(g, i)
                pool.wait_ge(v_free, g * STEPS + i + 1 + NDIAG - NV)
                pool.nop(nofuse=True)
                t, s = divmod(i, SLOTS)
                pool.indirect_dma_start(
                    v_rows[:, i % NV, :], None, peer_v,
                    bass.IndirectOffsetOnAxis(ap=ids_peer[:, t, s:s + 1], axis=0)).then_inc(v_in[i % NV], 16)

            def peer(g, last):
                for m in range(STEPS):
                    if has_slot(g, m + LEAD + AHEAD, last):
                        gather_u(g, m + LEAD + AHEAD)
                    if has_slot(g, m + LEAD, last):
                        gather_v(g, m + LEAD)

            peer(-1, False)
            with pool.Fori(0, GROUPS - 1) as g:
                peer(g, False)
            peer(GROUPS - 1, True)

        @block.tensor
        def _(pe):
            mm = nc.tensor.matmul

            def tr(out_, in_):
                return nc.tensor.transpose(out_, in_, ident[:, :])

            for _ in range(NDIAG):
                pe.nop().then_inc(v_free, 1)
            pe.wait_ge(consts_in, 16 * 8)
            for i in range(TT + 1):
                if i < TT:
                    pe.wait_ge(h0_done, i + 1)
                    if positive(i):
                        pe.wait_ge(h0T_sb, i)
                    for k in range(KD):
                        last = tr(fA[:, tok(k)], h_t[:, i % 2, tok(k)])
                    last.then_inc(h0T_ps, 1)
                if i >= 1:
                    j = i - 1
                    pe.wait_ge(lat_done, j + 1)
                    if positive(j):
                        pe.wait_ge(latT_sb, j)
                    for c in range(4):
                        last = tr(m1[:, tok(c)], c_t[:, j % 2, tok(c)])
                    last.then_inc(latT_ps, 1)
                if i < TT:
                    if i == 0:
                        pe.wait_ge(w_lat_in, 16)
                    pe.wait_ge(h0T_sb, i + 1)
                    if positive(i):
                        pe.wait_ge(lat_ms, i)
                    for k in range(KD):
                        last = mm(m0[:, :], hT_all[:, k, tok(i)], w_lat_sb[:, k, :], start=k == 0, stop=k == KD - 1)
                    last.then_inc(lat_ps, 1)
            pe.wait_ge(w_z_in, 32)
            for n in range(2 * FG):
                g, half = divmod(n, 2)
                if positive(n - 3):
                    pe.wait_ge(z_sb, n - 3)
                for k in range(KD):
                    last = mm(banks[n % 4], w_z_sb[:, k, g * FD:(g + 1) * FD], hT_all[:, k, half * 512:(half + 1) * 512],
                              start=k == 0, stop=k == KD - 1)
                last.then_inc(z_ps, 1)
            for _ in range(NW):
                pe.nop().then_inc(w_free, 1)
            pe.wait_ge(latT_sb, TT)
            for half in range(2):
                for k in range(KD):
                    last = mm((m0, m1)[half][64:128, :], w_kr_sb[:, k, :], hT_all[:, k, half * 512:(half + 1) * 512],
                              start=k == 0, stop=k == KD - 1)
                last.then_inc(kr_ps, 1)
            for n in range(TT * FG):
                tt, g = divmod(n, FG)
                if n == 0:
                    pe.wait_ge(hT_in, 16)
                if g == 0 or n == 0:
                    pe.wait_ge(z_sb, 2 * FG)
                if positive(n - 3):
                    pe.wait_ge(zc_sb[n % 2], n // 2 - 1)
                mm(banks[n % 4][:, 0:2 * FD], zT[:, g, tok(tt)], dftc, start=True, stop=True).then_inc(zc_ps, 1)
            pe.wait_ge(w_kv_in, 32)
            pe.wait_ge(kr_sb, 2)
            for n in range(H):
                pair, half = divmod(n, 2)
                if positive(n - 1):
                    pe.wait_ge(k_sb, n - 1)
                for k in range(2):
                    last = mm((m0, m1)[n % 2][:, :], w_uk_sb[:, k, tok(pair)], ckvT_all[:, k, half * 512:(half + 1) * 512],
                              start=k == 0, stop=k == 1)
                last.then_inc(k_ps, 1)
            pe.wait_ge(k_sb, H)
            for i in range(TT):
                if positive(i - 1):
                    pe.wait_ge(v_sb, i - 1)
                for k in range(2):
                    last = mm((m0, m1)[i % 2][:, :], ckvT_all[:, k, tok(i)], w_uv_sb[:, k, :], start=k == 0, stop=k == 1)
                last.then_inc(v_ps, 1)
            pe.wait_ge(keys_in, 16)
            pe.wait_ge(v_sb, TT)
            for b in range(4):
                if positive(b - 1):
                    pe.wait_ge(keys_sbuf, b - 1)
                for j in range(4):
                    last = tr((m0, m1)[b % 2][:, tok(j)], keys_sb[:, 4 * b + j, :])
                last.then_inc(keys_ps, 1)
            pe.wait_ge(keys_sbuf, 4)
            for e in range(2):
                pe.wait_ge(zc_sb[e], TT * FG // 2)
            pe.wait_ge(z_sum, 1)
            for g in range(FG):
                last = mm(m0[:, g:g + 1], zsum[:, g, :], altern[:, 0:1], start=True, stop=True)
            last.then_inc(y_mid, 1)
            pe.wait_ge(y_mid, 2)

            def chunk(g, c):
                pe.wait_ge(w_in_s[c % NW], g * (16 * CHUNKS // NW) + 16 * (c // NW + 1))
                return wring[:, c % NW, :]

            def front(g, m):
                for u in range(TILES * H):
                    a = A0 + A_PERIOD * u
                    qt, h = divmod(u, H)
                    if m == a and qt == 0:
                        c0 = WQ0 + 2 * (h // 4)
                        if h == 0:
                            pe.wait_ge(q_in, 32 * g + 32)
                        if h % 4 == 0:
                            chunk(g, c0)
                            chunk(g, c0 + 1)
                        if positive(g * H + h):
                            pe.wait_ge(q_nope, g * H + h)
                        if positive(g * H + h):
                            pe.wait_ge(q_rope, g * H + h)
                        if h == 0:
                            if positive(g * 2 * PH):
                                pe.wait_ge(s_sb, g * 2 * PH)
                        o = (h % 4) * P
                        for k in range(2):
                            last = mm(m0[:, 0:GROUP], wring[:, (c0 + k) % NW, o:o + P], cqT_g[:, k, :],
                                      start=k == 0, stop=k == 1)
                        last.then_inc(q_ps, 1)
                        if h % 4 == 3:
                            pe.drain().then_inc(w_free, 1)
                            pe.drain().then_inc(w_free, 1)
                    if m == a + 2:
                        if qt == 0:
                            pe.wait_ge(q_nope, g * H + h + 1)
                            pe.wait_ge(q_rope, g * H + h + 1)
                        if positive(g * TILES * H + u):
                            pe.wait_ge(probs_sb, g * TILES * H + u)
                        if u == 0:
                            if positive(g * TILES):
                                pe.wait_ge(h1T_sb, g * TILES)
                        for half in range(2):
                            last = mm(fA[:, half * 512:(half + 1) * 512], qT_g[0:QK, h, tok(qt)],
                                      KT[0:QK, h, half * 512:(half + 1) * 512], start=True, stop=True)
                        last.then_inc(scores_ps, 1)
                    if m == a + 5:
                        pe.wait_ge(probs_sb, g * TILES * H + u + 1)
                        if positive(g * TILES * H + u):
                            pe.wait_ge(probsT_sb, g * TILES * H + u)
                        for k in range(TT):
                            last = tr(fB[:, tok(k)], probs[:, tok(k)])
                        last.then_inc(probsT_ps, 1)
                    if m == a + 7:
                        pe.wait_ge(probsT_sb, g * TILES * H + u + 1)
                        if h == 0:
                            if positive(g * TILES + qt):
                                pe.wait_ge(o_done, g * TILES + qt)
                        for k in range(TT):
                            last = mm(m1[:, h * VD:(h + 1) * VD], probsT[:, tok(k)], V[:, k, h * VD:(h + 1) * VD],
                                      start=k == 0, stop=k == TT - 1)
                        last.then_inc(pv_ps, 1)
                    if h == H - 1 and m == a + 9:
                        pe.wait_ge(o_done, g * TILES + qt + 1)
                        if positive(g * TILES + qt):
                            pe.wait_ge(oT_sb, g * TILES + qt)
                        for c in range(4):
                            last = tr(m0[:, tok(c)], o_sb[:, tok(c)])
                        last.then_inc(oT_ps, 1)
                for dc in range(KD):
                    a = M0 + M_PERIOD * dc
                    gb, yb = banks[dc % 2], banks[2 + dc % 2]
                    for j in range(2):
                        if m == a + 2 * j:
                            if dc == 0 and j == 0:
                                pe.wait_ge(hT_in, 16 + 16 * (g + 1))
                                pe.wait_ge(probsT_sb, (g + 1) * TILES * H)
                            if j == 0:
                                if positive(g * KD + dc - 1):
                                    pe.wait_ge(gates_sb, g * KD + dc - 1)
                            w = chunk(g, WM0 + 3 * dc + j)
                            for k in range(KD):
                                last = mm(gb[:, j * GROUP:(j + 1) * GROUP], w[:, tok(k)], hT_g[:, k, :],
                                          start=k == 0, stop=k == KD - 1)
                            last.then_inc(w_free, 1)
                    if m == a + 4:
                        if dc == 0:
                            pe.wait_ge(yT_in, 16 * (g + 1))
                            pe.wait_ge(oT_sb, (g + 1) * TILES)
                        if positive(g * KD + dc - 1):
                            pe.wait_ge(m_done, g * KD + dc - 1)
                        w = chunk(g, WM0 + 3 * dc + 2)
                        for j, src in ((0, oT), (1, yT_g)):
                            for k in range(4):
                                last = mm(yb[:, j * GROUP:(j + 1) * GROUP], w[:, tok(4 * j + k)], src[:, k, :],
                                          start=k == 0, stop=k == 3)
                        last.then_inc(w_free, 1)
                for k in range(KD):
                    if m == O0 + 2 * k:
                        if k == 0:
                            pe.wait_ge(m_done, (g + 1) * KD)
                        w = chunk(g, WO0 + k)
                        for t in range(TILES):
                            for half in range(2):
                                last = mm(banks[2 * t + half], mT[:, k, tok(t)], w[:, half * 512:(half + 1) * 512],
                                          start=k == 0, stop=k == KD - 1)
                        last.then_inc(w_free, 1)
                for t in range(TILES):
                    if m == L0 + 4 + 4 * t:
                        pe.wait_ge(h1_done, g * TILES + t + 1)
                        for k in range(KD):
                            last = tr((fA, fB)[t][:, tok(k)], h1_front[:, t, tok(k)])
                        last.then_inc(h1T_ps, 1)
                for qc in range(2 * PH):
                    a = K0 + K_PERIOD * qc
                    if m == a:
                        if qc == 0:
                            pe.wait_ge(h1T_sb, (g + 1) * TILES)
                            pe.wait_ge(oT_sb, (g + 1) * TILES)
                        if positive(g * 2 * PH + qc - 1):
                            pe.wait_ge(qc_sb, g * 2 * PH + qc - 1)
                        w = chunk(g, WP0 + qc)
                        for k in range(KD):
                            last = mm(m0[:, (qc % 2) * GROUP:(qc % 2 + 1) * GROUP], w[:, tok(k)], hT_g[:, k, :],
                                      start=k == 0, stop=k == KD - 1)
                        last.then_inc(w_free, 1)
                    if m == a + 3:
                        pe.wait_ge(qc_sb, g * 2 * PH + qc + 1)
                        if positive(g * 2 * PH + qc - 1):
                            pe.wait_ge(s_sb, g * 2 * PH + qc - 1)
                        for t in range(TILES):
                            last = mm(m1[:, (qc % 2) * GROUP + t * P:(qc % 2) * GROUP + (t + 1) * P],
                                      qcT[:, qc % 2, tok(t)], keysT[:, qc, :], start=True, stop=True)
                        last.then_inc(s_ps, 1)

            def dft(m):
                if m % 2 == 1 and m < 2 * TT * FG:
                    n = m // 2
                    g, tt = divmod(n, TT)
                    if tt == 0 and g > 0:
                        pe.wait_ge(y_done, g)
                    pe.wait_ge(dft_in[n % NDFT], 16 * (n // NDFT + 1))
                    for cs, part in enumerate((cos_part, sin_part)):
                        last = mm(part, zcs[:, tt, g, cs * FD:(cs + 1) * FD], dft_ring[:, n % NDFT, cs, :],
                                  start=tt == 0, stop=tt == TT - 1)
                    last.then_inc(dft_used, 1)

            def peer(g, i):
                g, i = slot_of(g, i)
                if i % SLOTS == 0:
                    pe.wait_ge(acc_free, g * TILES + i // SLOTS + 1)
                if i % BATCH == 0:
                    pe.wait_ge(diag_done, g * STEPS + i + BATCH)
                pe.wait_ge(v_in[i % NV], g * (16 * STEPS // NV) + 16 * (i // NV + 1))
                for half in range(2):
                    last = mm(acc[:, half * 512:(half + 1) * 512], diag[:, i % NDIAG, :],
                              v_rows[:, i % NV, half * 512:(half + 1) * 512],
                              start=i % SLOTS == 0, stop=i % SLOTS == SLOTS - 1)
                last.then_inc(v_free, 1)

            for m in range(STEPS):
                if has_slot(-1, m + LEAD, False):
                    peer(-1, m + LEAD)
                front(0, m)
                dft(m)
            with pe.Fori(0, GROUPS - 1) as g:
                for m in range(STEPS):
                    peer(g, m + LEAD)
                    front(g + 1, m)
            for m in range(STEPS - LEAD):
                peer(GROUPS - 1, m + LEAD)

        @block.vector
        def _(dve):
            v = nc.vector

            def stats(n, src, var_ready):
                for half in range(2):
                    v.bn_stats(st[:, n, 6 * half:6 * half + 6], src[:, half * 512:(half + 1) * 512])
                dve.drain()
                v.bn_aggr(mv[:, n, :], st[:, n, :])
                dve.drain()
                v.tensor_scalar(sd[:, n, 0:1], mv[:, n, 1:2], LN_EPS, None, ALU.add).then_inc(var_ready, 1)

            def normalise(n, dst, src, std_ready, count, gamma, beta, done):
                v.scalar_tensor_tensor(out=dst, in0=src, scalar=mv[:, n, 0:1], in1=gamma, op0=ALU.subtract, op1=ALU.mult)
                dve.wait_ge(std_ready, count)
                v.reciprocal(sd[:, n, 0:1], sd[:, n, 1:2])
                dve.drain()
                last = v.scalar_tensor_tensor(out=dst, in0=dst, scalar=sd[:, n, 0:1], in1=beta, op0=ALU.mult, op1=ALU.add)
                if done is not None:
                    last.then_inc(done, 1)

            for _ in range(NU):
                dve.nop().then_inc(u_free, 1)
            dve.nop().then_inc(acc_free, 1)
            dve.wait_ge(ln0_in, 64)

            def latents(i):
                dve.wait_ge(lat_ps, i + 1)
                if positive(i - 1):
                    dve.wait_ge(latT_ps, i - 1)
                c = c_t[:, i % 2, :]
                v.tensor_tensor(c, m0[:, :], blat, ALU.add).then_inc(lat_ms, 1)
                dve.drain()
                for j in range(2):
                    v.tensor_tensor_reduce(out=ybuf[:, j * LORA:(j + 1) * LORA], in0=c[:, j * LORA:(j + 1) * LORA],
                                           in1=c[:, j * LORA:(j + 1) * LORA], scale=1.0, scalar=0.0,
                                           op0=ALU.mult, op1=ALU.add, accum_out=rq[:, j:j + 1])
                dve.drain()
                v.tensor_scalar(rq[:, 0:2], rq[:, 0:2], 1.0 / LORA, RMS_EPS, ALU.mult, ALU.add).then_inc(lat_rms, 1)
                dve.wait_ge(lat_rms, 2 * i + 2)
                v.reciprocal(rq[:, 0:2], rq[:, 2:4])
                dve.drain()
                v.tensor_scalar(c[:, 0:LORA], c[:, 0:LORA], rq[:, 0:1], None, ALU.mult)
                v.tensor_scalar(c[:, LORA:], c[:, LORA:], rq[:, 1:2], None, ALU.mult).then_inc(lat_done, 1)

            def stats0(i):
                dve.wait_ge(x_in[i % 2], 16 * (i // 2 + 1))
                stats(i % 2, x_t[:, i % 2, :], var0)

            stats0(0)
            for i in range(TT):
                if positive(i - 1):
                    dve.wait_ge(h0T_ps, i - 1)
                    dve.wait_ge(hres_made, i - 1)
                normalise(i % 2, h_t[:, i % 2, :], x_t[:, i % 2, :], std0, i + 1, ln0[:, 0, :], ln0[:, 1, :], h0_done)
                dve.drain()
                if i + 1 < TT:
                    stats0(i + 1)
                if i >= 1:
                    latents(i - 1)
            latents(TT - 1)
            dve.wait_ge(rope_in, 16)
            dve.wait_ge(consts_in, 16 * 8)
            for i in range(2):
                dve.wait_ge(hres_out[i], 16 * (TT // 2))
            dve.wait_ge(h0T_ps, TT)
            for half in range(2):
                cols = slice(half * 512, (half + 1) * 512)
                dve.wait_ge(kr_ps, half + 1)
                bank = (m0, m1)[half]
                v.scalar_tensor_tensor(out=rope_tmp[64:96, 0:512], in0=bank[64:96, :], scalar=bkr[64:96, 0:1],
                                       in1=rope_all[64:96, cols], op0=ALU.add, op1=ALU.mult)
                v.scalar_tensor_tensor(out=ybuf[64:96, 0:512], in0=bank[96:128, :], scalar=bkr[96:128, 0:1],
                                       in1=rope_all[96:128, cols], op0=ALU.add, op1=ALU.mult)
                dve.drain()
                v.tensor_tensor(KT[64:96, 0, cols], rope_tmp[64:96, 0:512], ybuf[64:96, 0:512],
                                ALU.add).then_inc(kr_sb, 1)
                dve.drain()
            for n in range(0, TT * FG, 2):
                tt, g = divmod(n, FG)
                dve.wait_ge(zc_ps, n + 1)
                v.tensor_copy(zcs[:, tt, g, :], banks[n % 4][:, 0:2 * FD]).then_inc(zc_sb[0], 1)
            dve.wait_ge(zc_sb[0], TT * FG // 2)
            dve.wait_ge(zc_sb[1], TT * FG // 2)
            v.reduce_sum(zsum, zcs[:, :, :, 0:FD].rearrange("p t g c -> p g c t"), AX).then_inc(z_sum, 1)
            dve.wait_ge(stored, 16)
            for i in range(TT):
                dve.wait_ge(v_ps, i + 1)
                v.tensor_copy(V[:, i, :], (m0, m1)[i % 2][:, :]).then_inc(v_sb, 1)
            for b in range(4):
                dve.wait_ge(keys_ps, b + 1)
                v.tensor_copy(keysT[:, 4 * b:4 * b + 4, :].rearrange("p a b -> p (a b)"),
                              (m0, m1)[b % 2][:, :]).then_inc(keys_sbuf, 1)
            dve.wait_ge(y_mid, 1)
            v.tensor_copy(ymid[:, :], m0[:, 0:FG]).then_inc(y_mid, 1)
            dve.drain()

            def topk(vals, val16, idx16):
                v.max(val16[:, 0:8], vals)
                dve.drain()
                v.max_index(idx16[:, 0:8], val16[:, 0:8], vals)
                dve.drain()
                v.match_replace(vals, val16[:, 0:8], vals, NEG)
                dve.drain()
                v.max(val16[:, 8:16], vals)
                dve.drain()
                v.max_index(idx16[:, 8:16], val16[:, 8:16], vals)

            def front(g, m):
                for u in range(TILES * H):
                    a = A0 + A_PERIOD * u
                    qt, h = divmod(u, H)
                    if m == a and qt == 0:
                        dve.wait_ge(q_ps, g * H + h + 1)
                        if h == 0:
                            dve.wait_ge(q_in, 32 * g + 32)
                        v.tensor_tensor(prod[64:96, 0, :], m0[64:96, 0:GROUP], rope_g[64:96, :], ALU.mult)
                        v.tensor_tensor(prod[64:96, 1, :], m0[96:128, 0:GROUP], rope_g[96:128, :], ALU.mult)
                        dve.drain()
                        v.tensor_tensor(qT_g[64:96, h, :], prod[64:96, 0, :], prod[64:96, 1, :],
                                        ALU.add).then_inc(q_rope, 1)
                        dve.drain()
                    if m == a + 2:
                        dve.wait_ge(scores_ps, g * TILES * H + u + 1)
                        v.reduce_max(nmax[:, u % 2:u % 2 + 1], fA[:, :], AX)
                        dve.drain()
                        v.tensor_scalar(nmax[:, u % 2:u % 2 + 1], nmax[:, u % 2:u % 2 + 1], -(QK ** -0.5), None,
                                        ALU.mult).then_inc(row_max, 1)
                    if m == a + 5:
                        dve.wait_ge(probsT_ps, g * TILES * H + u + 1)
                        if positive(g * TILES * H + u):
                            dve.wait_ge(pv_ps, g * TILES * H + u)
                        v.tensor_copy(probsT, fB[:, :]).then_inc(probsT_sb, 1)
                    if h == H - 1 and m == a + 8:
                        dve.wait_ge(pv_ps, g * TILES * H + u + 1)
                        if positive(g * TILES + qt):
                            dve.wait_ge(oT_ps, g * TILES + qt)
                        v.reciprocal(rrow[:, qt, :], rowsum[:, qt, :])
                        dve.drain()
                        v.tensor_tensor(o_sb[:, :].rearrange("p (h d) -> p h d", h=H),
                                        m1[:, :].rearrange("p (h d) -> p h d", h=H),
                                        rrow[:, qt, :].unsqueeze(2).to_broadcast([P, H, VD]),
                                        ALU.mult).then_inc(o_done, 1)
                for dc in range(KD):
                    if m == M0 + M_PERIOD * dc + 5:
                        dve.wait_ge(gates_sb, g * KD + dc + 1)
                        dve.wait_ge(w_free, used(g, WM0 + 3 * dc + 2))
                        v.tensor_tensor(prod[:, :, :].rearrange("p a b -> p (a b)"),
                                        sg[:, :, :].rearrange("p a b -> p (a b)"), banks[2 + dc % 2], ALU.mult)
                        dve.drain()
                        v.tensor_tensor(mT[:, dc, :], prod[:, 0, :], prod[:, 1, :], ALU.add).then_inc(m_done, 1)
                        dve.drain()
                for t in range(TILES):
                    if m == L0 + 4 * t:
                        if t == 0:
                            dve.wait_ge(w_free, used(g, WP0 - 1))
                            dve.wait_ge(hres_in, 16 * (g + 1))
                        v.tensor_tensor(h1_front[:, t, :], h1_front[:, t, :], (fA, fB)[t][:, :], ALU.add)
                        dve.drain()
                        stats(1, h1_front[:, t, :], var1)
                    if m == L0 + 4 * t + 2:
                        normalise(1, h1_front[:, t, :], h1_front[:, t, :], std1, g * TILES + t + 1,
                                  ln[:, 0, :], ln[:, 1, :], h1_done)
                retrieve(g, 0, m, T0, T_PERIOD)

            def retrieve(g, t, m, t0, period):
                for h in range(PH):
                    a = t0 + period * h
                    for c in range(2):
                        if m == a + c:
                            if c == 0:
                                dve.wait_ge(s_sb, g * 2 * PH + 2 * h + 2)
                                dve.nop(nofuse=True)
                            topk(S2[:, t, 2 * h + c, :], sv[:, t, 2 * h + c, :], si[:, t, 2 * h + c, :])
                    if m == a + 2:
                        dve.drain()
                        cand = S2[:, t, 2 * h:2 * h + 2, :].rearrange("p a b -> p (a b)")
                        v.tensor_tensor(cand.rearrange("p (i j) -> p i j", i=TOPK),
                                        sv[:, t, 2 * h, :].unsqueeze(2).to_broadcast([P, TOPK, TOPK]),
                                        sv[:, t, 2 * h + 1, :].unsqueeze(1).to_broadcast([P, TOPK, TOPK]), ALU.add)
                        dve.drain()
                        topk(cand, cv[:, t, h, :], ci[:, t, h, :])
                for q in range(PAIRS):
                    a = t0 + period * (2 * q + 1) + IDS
                    heads, part = slice(2 * q, 2 * q + 2), slice(q * PSLOTS, (q + 1) * PSLOTS)
                    gates = gate_front[:, t, part].rearrange("p (h k) -> p h k", h=2)
                    if m == a:
                        places = ci[:, t, heads, :].rearrange("p a b -> p (a b)")
                        lists = slice(4 * q, 4 * q + 4)
                        dve.drain()
                        v.tensor_tensor(gates, cv[:, t, heads, :], cv[:, t, heads, 0:1].to_broadcast([P, 2, TOPK]),
                                        ALU.subtract).then_inc(gmax_done, 1)
                        v.tensor_copy(sv[:, t, lists, :], si[:, t, lists, :])
                        v.tensor_single_scalar(cabi[:, 0, :], places, 4, op=ALU.logical_shift_right)
                        v.tensor_single_scalar(cabi[:, 1, :], places, 15, op=ALU.bitwise_and)
                        dve.drain()
                        v.tensor_copy(cab[:, :, :], cabi[:, :, :])
                    for c in range(2):
                        if m == a + 1 + c:
                            dve.drain()
                            v.tensor_tensor(onehot[:, :, :], cab[:, c, :].unsqueeze(2).to_broadcast([P, PSLOTS, TOPK]),
                                            iota16[:, :].unsqueeze(1).to_broadcast([P, PSLOTS, TOPK]), ALU.is_equal)
                            dve.drain()
                            for h in range(2):
                                oh = onehot[:, h * TOPK:(h + 1) * TOPK, :]
                                number = sv[:, t, 2 * (2 * q + h) + c, :]
                                v.tensor_tensor(oh, oh, number.unsqueeze(1).to_broadcast([P, TOPK, TOPK]), ALU.mult)
                            dve.drain()
                            v.reduce_sum(cab[:, c, :], onehot[:, :, :], AX)
                    if m == a + 3:
                        dve.drain()
                        v.scalar_tensor_tensor(out=ids_peer[:, t, part], in0=cab[:, 0, :], scalar=float(NK),
                                               in1=cab[:, 1, :], op0=ALU.mult, op1=ALU.add).then_inc(handed, 1)
                        if q == 0:
                            v.tensor_copy(h1_peer[:, t, :], h1_front[:, t, :]).then_inc(h1_handed, 1)
                        dve.wait_ge(gexp_done, (g * TILES + t) * PAIRS + q + 1)
                        v.reduce_sum(gsum[:, :], gates, AX)
                        dve.drain()
                        v.reciprocal(gsum[:, :], gsum[:, :])
                        dve.drain()
                        v.tensor_tensor(gate_peer[:, t, part].rearrange("p (h k) -> p h k", h=2), gates,
                                        gsum[:, :].unsqueeze(2).to_broadcast([P, 2, TOPK]), ALU.mult)
                        dve.drain()

            def dot(g, i):
                g, i = slot_of(g, i)
                t = i // SLOTS
                dve.wait_ge(u_in[i % NU], g * (16 * STEPS // NU) + 16 * (i // NU + 1))
                row = u_rows[:, i % NU, :]
                b = i // BATCH % 2
                v.tensor_tensor_reduce(out=row, in0=row, in1=h1_peer[:, t, :], scale=1.0, scalar=0.0, op0=ALU.mult,
                                       op1=ALU.add, accum_out=dots[:, b, i % BATCH:i % BATCH + 1]).then_inc(u_free, 1)

            def diags(g, k):
                g, i = slot_of(g, k * BATCH)
                k = i // BATCH
                dve.wait_ge(act_done, g * (STEPS // BATCH) + k + 1)
                dve.wait_ge(v_free, g * STEPS + BATCH * k + BATCH)
                t, s0 = divmod(k * BATCH, SLOTS)
                for s in range(BATCH):
                    v.tensor_scalar(diag[:, (k * BATCH + s) % NDIAG, :], ident[:, :], act_out[:, k % 2, s:s + 1],
                                    gate_peer[:, t, s0 + s:s0 + s + 1], ALU.mult, ALU.mult).then_inc(diag_done, 1)

            def finish(g, t):
                dve.wait_ge(stored, 16 * (g * TILES + t) + 16)
                dve.wait_ge(v_free, g * STEPS + NDIAG + (t + 1) * SLOTS)
                v.scalar_tensor_tensor(out=ybuf[:, :], in0=h1_peer[:, t, :], scalar=ALPHA, in1=acc[:, :],
                                       op0=ALU.mult, op1=ALU.add).then_inc(acc_free, 1)
                dve.drain()
                stats(2, ybuf, var2)

            def finish_norm(g, t):
                normalise(2, ybuf[:, :], ybuf[:, :], std2, g * TILES + t + 1, ln[:, 2, :], ln[:, 3, :], out_ready)
                dve.drain()

            def peer(g, m, last):
                if has_slot(g, m + LEAD + AHEAD, last):
                    dot(g, m + LEAD + AHEAD)
                if m % BATCH == 5 and has_slot(g, m + LEAD + BATCH, last):
                    diags(g, (m + LEAD) // BATCH + 1)

            def dft(m):
                if m % (2 * TT) == 2 * TT - 1 and m < 2 * TT * FG:
                    g = m // (2 * TT)
                    dve.wait_ge(dft_used, TT * (g + 1))
                    if g >= 2:
                        dve.wait_ge(y_spilled[g % 2], 16)
                    y = y_part[:, g % 2, :]
                    v.tensor_copy(y[:, S // 2:S // 2 + 1], ymid[:, g:g + 1])
                    v.tensor_copy(ybuf[:, 0:512], sin_part)
                    dve.drain()
                    v.tensor_tensor(y[:, 0:512], cos_part, ybuf[:, 0:512], ALU.add)
                    v.tensor_tensor(y[:, S - 1:S // 2:-1], cos_part[:, 1:512], ybuf[:, 1:512],
                                    ALU.subtract).then_inc(y_done, 1)
                    dve.drain()

            for m in range(STEPS):
                if m == L0:
                    dve.wait_ge(ln_in, 64)
                peer(-1, m, False)
                front(0, m)
                dft(m)

            def group(g, last):
                for m in range(STEPS):
                    peer(g, m, last)
                    for t in range(TILES):
                        if m + LEAD == (t + 1) * SLOTS:
                            finish(g, t)
                        if m + LEAD == (t + 1) * SLOTS + 2:
                            finish_norm(g, t)
                    retrieve(g, 1, m, R0, R_PERIOD)
                    if not last:
                        front(g + 1, m)

            with dve.Fori(0, GROUPS - 1) as g:
                group(g, False)
            group(GROUPS - 1, True)

        @block.scalar
        def _(act):
            s = nc.scalar

            act.wait_ge(consts_in, 16 * 8)

            def load_queries(g):
                act.dma_start(cqT_g[:, :, :], cqT_d[:, :, bass.ds(g * GROUP, GROUP)]).then_inc(q_in, 16)
                act.dma_start(rope_g[64:128, :], rope_tab[:, bass.ds(g * GROUP, GROUP)]).then_inc(q_in, 16)

            def latent_cols(i):
                act.wait_ge(latT_ps, i + 1)
                for c in range(4):
                    dst = (cqT_all, ckvT_all)[c // 2][:, c % 2, tok(i)]
                    last = s.activation(dst, m1[:, tok(c)], ACT.Copy, scale=gqk[:, c // 2, c % 2:c % 2 + 1])
                last.then_inc(latT_sb, 1)

            def sqrt0(i):
                act.wait_ge(var0, i + 1)
                s.activation(sd[:, i % 2, 1:2], sd[:, i % 2, 0:1], ACT.Sqrt).then_inc(std0, 1)

            for i in range(TT + 1):
                if i == 0:
                    sqrt0(0)
                if i >= 1:
                    act.wait_ge(lat_rms, 2 * i - 1)
                    s.activation(rq[:, 2:4], rq[:, 0:2], ACT.Sqrt).then_inc(lat_rms, 1)
                if i < TT:
                    act.wait_ge(h0T_ps, i + 1)
                    s.activation(hT_all[:, :, tok(i)], fA[:, :].rearrange("p (k t) -> p k t", k=KD),
                                 ACT.Copy).then_inc(h0T_sb, 1)
                if i + 1 < TT:
                    sqrt0(i + 1)
                if i >= 1:
                    latent_cols(i - 1)
                if i < TT:
                    act.wait_ge(hres_sum, i + 1)
                    act.dma_start(hres_d[tok(i), :], hres_t[:, i % 2, :]).then_inc(hres_out[i % 2], 16)
            act.drain()
            act.dma_start(hT_d, hT_all[:, :, :]).then_inc(hT_in, 16)
            act.dma_start(cqT_d, cqT_all).then_inc(stored, 16)
            for n in range(2 * FG):
                g, half = divmod(n, 2)
                act.wait_ge(z_ps, n + 1)
                s.activation(zT[:, g, half * 512:(half + 1) * 512], banks[n % 4], ACT.Identity,
                             bias=bz[:, g:g + 1]).then_inc(z_sb, 1)
            act.wait_ge(stored, 16)
            load_queries(0)
            for n in range(1, TT * FG, 2):
                tt, g = divmod(n, FG)
                act.wait_ge(zc_ps, n + 1)
                s.activation(zcs[:, tt, g, :], banks[n % 4][:, 0:2 * FD], ACT.Copy).then_inc(zc_sb[1], 1)
            act.wait_ge(kr_sb, 2)
            for n in range(H):
                pair, half = divmod(n, 2)
                act.wait_ge(k_ps, n + 1)
                for odd in range(2):
                    last = s.activation(KT[0:NOPE, 2 * pair + odd, half * 512:(half + 1) * 512],
                                        (m0, m1)[n % 2][odd * NOPE:(odd + 1) * NOPE, :], ACT.Copy)
                last.then_inc(k_sb, 1)
            for i in range(2):
                act.wait_ge(hres_out[i], 16 * (TT // 2))
            act.wait_ge(hT_in, 16)
            act.wait_ge(kr_all, H - 1)
            act.wait_ge(v_ps, TT)
            for n in range(NDFT):
                act.dma_start(dft_ring[:, n, :, :],
                              dft_seq[:, tok(n), :].rearrange("m p n -> p m n")).then_inc(dft_in[n], 16)

            def front(g, m):
                if m == 0 and positive(g):
                    act.wait_ge(handed, (g * TILES - 1) * PAIRS)
                    load_queries(g)
                for u in range(TILES * H):
                    a = A0 + A_PERIOD * u
                    qt, h = divmod(u, H)
                    if m == a and qt == 0:
                        act.wait_ge(q_ps, g * H + h + 1)
                        s.activation(qT_g[0:NOPE, h, :], m0[0:NOPE, 0:GROUP], ACT.Copy).then_inc(q_nope, 1)
                    if m == a + 3:
                        act.wait_ge(row_max, g * TILES * H + u + 1)
                        if positive(g * TILES * H + u):
                            act.wait_ge(probsT_ps, g * TILES * H + u)
                        s.activation(probs, fA[:, :], ACT.Exp, bias=nmax[:, u % 2:u % 2 + 1], scale=QK ** -0.5,
                                     accum_out=rowsum[:, qt, h:h + 1]).then_inc(probs_sb, 1)
                    if h == H - 1 and m == a + 10:
                        act.wait_ge(oT_ps, g * TILES + qt + 1)
                        s.activation(oT[:, :, tok(qt)], m0[:, :].rearrange("p (c t) -> p c t", c=4),
                                     ACT.Copy).then_inc(oT_sb, 1)
                if m == A0 + A_PERIOD * (TILES * H - 1) + 3:
                    act.wait_ge(scores_ps, (g + 1) * TILES * H)
                    act.dma_start(hT_g[:, :, :], hT_d[:, :, bass.ds(g * GROUP, GROUP)]).then_inc(hT_in, 16)
                if m == M0 - 3:
                    act.dma_start(yT_g, yT_d[:, :, bass.ds(g * GROUP, GROUP)]).then_inc(yT_in, 16)
                for dc in range(KD):
                    if m == M0 + M_PERIOD * dc + 3:
                        act.wait_ge(w_free, used(g, WM0 + 3 * dc + 1))
                        if positive(g * KD + dc):
                            act.wait_ge(m_done, g * KD + dc)
                        for j in range(2):
                            last = s.activation(sg[:, j, :], banks[dc % 2][:, j * GROUP:(j + 1) * GROUP], ACT.Sigmoid,
                                                bias=bg[:, j, dc:dc + 1])
                        last.then_inc(gates_sb, 1)
                if m == HAND1 + 2:
                    if positive(2 * g):
                        act.wait_ge(h1_handed, 2 * g)
                    act.dma_start(h1_front, hres_d[bass.ds(g * GROUP, GROUP), :].rearrange("(t p) d -> p t d", p=P)
                                  ).then_inc(hres_in, 16)
                for t in range(TILES):
                    if m == L0 + 4 * t + 1:
                        act.wait_ge(var1, g * TILES + t + 1)
                        s.activation(sd[:, 1, 1:2], sd[:, 1, 0:1], ACT.Sqrt).then_inc(std1, 1)
                    if m == L0 + 4 * t + 6:
                        act.wait_ge(h1T_ps, g * TILES + t + 1)
                        s.activation(hT_g[:, :, tok(t)], (fA, fB)[t][:, :].rearrange("p (k t) -> p k t", k=KD),
                                     ACT.Copy).then_inc(h1T_sb, 1)
                for qc in range(2 * PH):
                    a = K0 + K_PERIOD * qc
                    if m == a + 1:
                        act.wait_ge(w_free, used(g, WP0 + qc))
                        if positive(g * 2 * PH + qc - 1):
                            act.wait_ge(s_ps, g * 2 * PH + qc - 1)
                        s.activation(qcT[:, qc % 2, :], m0[:, (qc % 2) * GROUP:(qc % 2 + 1) * GROUP],
                                     ACT.Copy).then_inc(qc_sb, 1)
                    if m == a + 4:
                        act.wait_ge(s_ps, g * 2 * PH + qc + 1)
                        s.activation(S2[:, :, qc, :],
                                     m1[:, (qc % 2) * GROUP:(qc % 2 + 1) * GROUP].rearrange("p (t n) -> p t n", t=TILES),
                                     ACT.Copy).then_inc(s_sb, 1)
                gate_exp(g, 0, m, T0, T_PERIOD)

            def gate_exp(g, t, m, t0, period):
                for q in range(PAIRS):
                    part = slice(q * PSLOTS, (q + 1) * PSLOTS)
                    if m == t0 + period * (2 * q + 1) + IDS + 1:
                        act.wait_ge(gmax_done, (g * TILES + t) * PAIRS + q + 1)
                        s.activation(gate_front[:, t, part], gate_front[:, t, part], ACT.Exp).then_inc(gexp_done, 1)

            def gelu(g, k):
                g, i = slot_of(g, k * BATCH)
                k = i // BATCH
                act.wait_ge(u_free, g * STEPS + NU + BATCH * (k + 1))
                s.activation(act_out[:, k % 2, :], dots[:, k % 2, :], ACT.Gelu).then_inc(act_done, 1)

            def finish(g, t):
                act.wait_ge(var2, g * TILES + t + 1)
                s.activation(sd[:, 2, 1:2], sd[:, 2, 0:1], ACT.Sqrt).then_inc(std2, 1)

            def store(g, t):
                act.wait_ge(out_ready, g * TILES + t + 1)
                act.dma_start(out[bass.ds(g * GROUP + t * P, P), :], ybuf[:, :]).then_inc(stored, 16)

            def dft(m):
                n = m // 2 - 1 + NDFT
                if m % 2 == 0 and NDFT <= n < TT * FG:
                    act.wait_ge(dft_used, n - NDFT + 1)
                    act.dma_start(dft_ring[:, n % NDFT, :, :],
                                  dft_seq[:, tok(n % TT), :].rearrange("m p n -> p m n")).then_inc(dft_in[n % NDFT], 16)
                if m % (2 * TT) == 1 and 0 < m // (2 * TT) <= FG:
                    g = m // (2 * TT) - 1
                    act.wait_ge(y_done, g + 1)
                    act.dma_start(yT_d[:, g, :], y_part[:, g % 2, :]).then_inc(y_spilled[g % 2], 16)
                if m == 2 * TT * FG + 2:
                    for j in range(4):
                        act.dma_start(ln[:, j, :], lnp[3 + j:4 + j, :].to_broadcast([P, D])).then_inc(ln_in, 16)
                    for i in range(2):
                        act.wait_ge(y_spilled[i], 16 * (FG // 2))

            def gelus(g, m, last):
                if m % BATCH == 4 and has_slot(g, m + LEAD + BATCH, last):
                    gelu(g, (m + LEAD) // BATCH + 1)

            for m in range(STEPS):
                gelus(-1, m, False)
                front(0, m)
                dft(m)

            def group(g, last):
                for m in range(STEPS):
                    gelus(g, m, last)
                    gate_exp(g, 1, m, R0, R_PERIOD)
                    if not last:
                        front(g + 1, m)
                    for t in range(TILES):
                        if m + LEAD == (t + 1) * SLOTS:
                            finish(g, t)
                        if m + LEAD == (t + 1) * SLOTS + 2:
                            store(g, t)

            with act.Fori(0, GROUPS - 1) as g:
                group(g, False)
            group(GROUPS - 1, True)
            act.wait_ge(stored, 16 * (TT + 1))


def kernel(**inputs):
    from concourse import bacc
    from concourse.bass_utils import run_bass_kernel_spmd

    f = {n: np.asarray(a) for n, a in inputs.items()}
    w_in, b_in = f["w_in"][0], f["b_in"][0]
    kr0, z0, g0 = 2 * LORA, 2 * LORA + ROPE, 2 * LORA + ROPE + FG * FD

    def blocks(w):
        return np.ascontiguousarray(w.reshape(-1, P, w.shape[-1]).transpose(1, 0, 2))

    swap = np.r_[ROPE // 2:ROPE, 0:ROPE // 2]
    w_kr = w_in[:, kr0:z0]
    b_kr = b_in[kr0:z0]
    uq = f["w_uq"][0].reshape(2, P, H, QK)
    uq = np.concatenate([uq, uq[..., NOPE + swap]], axis=-1)
    chunks = []
    for half in range(2):
        for k in range(2):
            c = uq[k, :, 4 * half:4 * half + 4].reshape(P, 512)
            chunks.append(np.concatenate([c, c], axis=1))
    wo, wf = blocks(f["w_o_attn"][0]), blocks(f["w_fourier"][0])
    gw = blocks(w_in[:, g0:])
    for dc in range(KD):
        cols = slice(dc * P, (dc + 1) * P)
        for j in range(2):
            chunks.append(gw[:, :, j * D + dc * P:j * D + (dc + 1) * P].reshape(P, D))
        chunks.append(np.concatenate([wo[:, :, cols], wf[:, :, cols]], axis=1).reshape(P, D))
    chunks += list(f["w_out"][0].reshape(KD, P, D))
    wq = blocks(f["peer_w_q"][0])
    for qc in range(2 * PH):
        chunks.append(wq[:, :, qc * P:(qc + 1) * P].reshape(P, D))

    pos = np.arange(S, dtype=np.float32)
    inv = (1.0 / (np.float32(10000.0) ** (np.arange(0, ROPE, 2, dtype=np.float32) / ROPE))).astype(np.float32)
    ang = (pos[None, :] * inv[:, None]).astype(np.float32)
    cos, sin = np.cos(ang), np.sin(ang)
    rope = np.concatenate([cos, cos, -sin, sin]).astype(np.float32)
    n = np.arange(S)
    w = 2 * math.pi * ((n[:, None] * n[None, :]) % S) / S
    dft_seq = np.stack([np.cos(w), np.sin(w)])[:, :, :S // 2].astype(np.float32)
    c = np.arange(FD)
    w = 2 * math.pi * ((c[:, None] * c[None, :]) % FD) / FD
    dft_ch = (np.concatenate([np.cos(w), -np.sin(w)], axis=1) / math.sqrt(S * FD)).astype(np.float32)

    arrays = {
        "x": f["x"][0],
        "lnp": np.stack([f["ln0_g"], f["ln0_b"], f["b_out"][0], f["ln1_g"][0], f["ln1_b"][0],
                         f["ln2_g"][0], f["ln2_b"][0]]),
        "w_lat": blocks(w_in[:, :kr0]),
        "w_z": blocks(w_in[:, z0:g0]),
        "w_kr": blocks(np.concatenate([w_kr, w_kr[:, swap]], axis=1)),
        "b_lat": b_in[None, :kr0],
        "b_zT": b_in[z0:g0].reshape(FG, FD).T,
        "b_krT": np.concatenate([b_kr, b_kr[swap]])[:, None],
        "gqkv": np.stack([f["q_norm_g"][0].reshape(2, P), f["kv_norm_g"][0].reshape(2, P)]).transpose(2, 0, 1),
        "w_uk": blocks(f["w_uk"][0]),
        "w_uv": blocks(f["w_uv"][0]),
        "b_gate": b_in[g0:].reshape(2, KD, P).transpose(2, 0, 1),
        "wstream": np.stack(chunks),
        "peer_keys": f["peer_keys"][0].reshape(2 * PH, NK, HALF),
        "peer_u": f["peer_w_u"][0],
        "peer_v": f["peer_w_v"][0],
        "ident_in": np.eye(P, dtype=np.float32),
        "dft_seq": dft_seq,
        "dft_ch": dft_ch,
        "rope_tab": rope,
        "iota_in": np.tile(np.arange(TOPK, dtype=np.float32), (P, 1)),
        "altern_in": (1.0 - 2.0 * (np.arange(P) % 2)).astype(np.float32)[:, None],
    }
    nc = bacc.Bacc("TRN2", target_bir_lowering=False, num_devices=1)
    args, feeds = [], {}
    for name, a in arrays.items():
        a = np.ascontiguousarray(a)
        feeds[f"in_{name}"] = a
        args.append(nc.dram_tensor(f"in_{name}", a.shape, mybir.dt.from_np(a.dtype), kind="ExternalInput").ap())
    args.append(nc.dram_tensor("out_h", (S, D), mybir.dt.float32, kind="ExternalOutput").ap())
    layer_program(nc, *args)
    r = run_bass_kernel_spmd(nc, [feeds], core_ids=[0])
    return r.results[0]["out_h"].reshape(1, S, D)
```
